# Optimizing a Trainium2 kernel written in Bass

```python
import jax, jax.numpy as jnp
from jax import lax
import numpy as np

D_MODEL = 1024
BATCH = 1
SEQ = 2048
DEPTH = 1

RET_HEADS = 4
RET_DK = 128
RET_DV = 128
RET_WIDTH = RET_HEADS * RET_DV
RET_CHUNK = 128

ATT_HEADS = 8
ATT_KV_HEADS = 2
ATT_HEAD_DIM = 64
ATT_WIDTH = ATT_HEADS * ATT_HEAD_DIM
ATT_KV_WIDTH = ATT_KV_HEADS * ATT_HEAD_DIM
WINDOW = 128
ATT_BLOCK = 128

D_MIX = RET_WIDTH + ATT_WIDTH
SPLIT_SIZES = (RET_HEADS * RET_DK, RET_HEADS * RET_DK, RET_WIDTH, RET_WIDTH,
               ATT_WIDTH, ATT_KV_WIDTH, ATT_KV_WIDTH, ATT_WIDTH)
IN_COLS = sum(SPLIT_SIZES)
EPS = 1e-6
NEG_BIG = -1e30

kernel_name = "hymba_retention_swa_sink_sandwich"

def rms_norm(x, g):
    xf = x.astype(jnp.float32)
    y = xf * lax.rsqrt(jnp.mean(xf * xf, axis=-1, keepdims=True) + EPS)
    return (y * g.astype(jnp.float32)).astype(x.dtype)

def retention(q, k, v):
    bsz, seq, nh, dk = q.shape
    dv = v.shape[-1]
    c = RET_CHUNK
    nc = seq // c
    f32 = jnp.float32
    log_gamma = jnp.log1p(-jnp.exp2(-5.0 - jnp.arange(nh, dtype=f32)))
    pos = jnp.arange(c, dtype=f32)
    diff = pos[:, None] - pos[None, :]
    intra_decay = jnp.where(diff >= 0,
                            jnp.exp(log_gamma[:, None, None] * jnp.maximum(diff, 0.0)),
                            0.0)
    xi = jnp.exp(log_gamma[:, None] * (pos + 1.0))
    zeta = jnp.exp(log_gamma[:, None] * (c - 1.0 - pos))
    chunk_decay = jnp.exp(log_gamma * c)

    qc = q.astype(f32).reshape(bsz, nc, c, nh, dk)
    kc = k.astype(f32).reshape(bsz, nc, c, nh, dk) * (dk ** -0.5)
    vc = v.astype(f32).reshape(bsz, nc, c, nh, dv)

    scores = jnp.einsum('bnihd,bnjhd->bnhij', qc, kc) * intra_decay
    inner = jnp.einsum('bnhij,bnjhe->bnihe', scores, vc)
    kv = jnp.einsum('bnjhd,hj,bnjhe->bnhde', kc, zeta, vc)

    def step(state, kv_c):
        return chunk_decay[None, :, None, None] * state + kv_c, state

    _, prev = lax.scan(step, jnp.zeros((bsz, nh, dk, dv), f32), jnp.moveaxis(kv, 1, 0))
    prev = jnp.moveaxis(prev, 0, 1)
    cross = jnp.einsum('bnihd,hi,bnhde->bnihe', qc, xi, prev)
    o = (inner + cross).reshape(bsz, seq, nh, dv)
    mu = jnp.mean(o, axis=-1, keepdims=True)
    var = jnp.mean(jnp.square(o - mu), axis=-1, keepdims=True)
    o = (o - mu) * lax.rsqrt(var + EPS)
    return o.reshape(bsz, seq, nh * dv).astype(q.dtype)

def swa_sink_attention(q, k, v, sinks):
    bsz, seq, hq, d = q.shape
    hkv = k.shape[2]
    grp = hq // hkv
    t = ATT_BLOCK
    nb = seq // t
    f32 = jnp.float32
    qb = q.reshape(bsz, nb, t, hkv, grp, d)
    kb = k.reshape(bsz, nb, t, hkv, d)
    vb = v.reshape(bsz, nb, t, hkv, d)
    pad = ((0, 0), (1, 0), (0, 0), (0, 0), (0, 0))
    kk = jnp.concatenate([jnp.pad(kb, pad)[:, :-1], kb], axis=2)
    vv = jnp.concatenate([jnp.pad(vb, pad)[:, :-1], vb], axis=2)

    s = jnp.einsum('bnqhgd,bnkhd->bnhgqk', qb, kk).astype(f32) * (d ** -0.5)
    qpos = jnp.arange(t) + t
    kpos = jnp.arange(2 * t)
    dist = qpos[:, None] - kpos[None, :]
    blk = jnp.arange(nb)
    valid = ((dist >= 0) & (dist < WINDOW))[None] & \
        ((blk[:, None, None] > 0) | (kpos[None, None, :] >= t))
    slopes = jnp.exp2(-8.0 * (jnp.arange(hq, dtype=f32) + 1.0) / hq).reshape(hkv, grp)
    s = s - slopes[:, :, None, None] * dist.astype(f32)
    s = jnp.where(valid[None, :, None, None], s, NEG_BIG)
    sink = jnp.broadcast_to(sinks.astype(f32).reshape(1, 1, hkv, grp, 1, 1),
                            s.shape[:-1] + (1,))
    p = jax.nn.softmax(jnp.concatenate([s, sink], axis=-1), axis=-1)[..., :-1]
    o = jnp.einsum('bnhgqk,bnkhd->bnqhgd', p.astype(v.dtype), vv)
    return o.reshape(bsz, seq, hq * d)

def setup_inputs(seed: int = 0) -> dict:
    key = jax.random.key(seed)
    ks = jax.random.split(key, 7)
    x = jax.random.normal(ks[0], (BATCH, SEQ, D_MODEL), jnp.float32)
    g_pre = 1.0 + 0.02 * jax.random.normal(ks[1], (D_MODEL,), jnp.float32)
    w_in = jax.random.normal(ks[2], (D_MODEL, IN_COLS), jnp.float32) * D_MODEL ** -0.5
    sinks = 0.5 * jax.random.normal(ks[3], (ATT_HEADS,), jnp.float32)
    w_out = jax.random.normal(ks[4], (D_MIX, D_MODEL), jnp.float32) * D_MIX ** -0.5
    g_post = 1.0 + 0.02 * jax.random.normal(ks[5], (D_MODEL,), jnp.float32)
    return {"x": x, "g_pre": g_pre, "w_in": w_in, "sinks": sinks,
            "w_out": w_out, "g_post": g_post}

def reference(x, g_pre, w_in, sinks, w_out, g_post):
    bsz, seq, _ = x.shape
    for _layer in range(DEPTH):
        h = rms_norm(x, g_pre)
        proj = jnp.einsum('bsd,dc->bsc', h, w_in)
        bounds = list(np.cumsum(SPLIT_SIZES)[:-1])
        rq, rk, rv, rg, aq, ak, av, ag = jnp.split(proj, bounds, axis=-1)
        ret = retention(rq.reshape(bsz, seq, RET_HEADS, RET_DK),
                        rk.reshape(bsz, seq, RET_HEADS, RET_DK),
                        rv.reshape(bsz, seq, RET_HEADS, RET_DV))
        ret = ret * jax.nn.silu(rg)
        att = swa_sink_attention(aq.reshape(bsz, seq, ATT_HEADS, ATT_HEAD_DIM),
                                 ak.reshape(bsz, seq, ATT_KV_HEADS, ATT_HEAD_DIM),
                                 av.reshape(bsz, seq, ATT_KV_HEADS, ATT_HEAD_DIM),
                                 sinks)
        att = att * jax.nn.silu(ag)
        mixed = jnp.concatenate([ret, att], axis=-1)
        out = jnp.einsum('bsc,cd->bsd', mixed, w_out)
        x = x + rms_norm(out, g_post)
    return x


_drawn_inputs = setup_inputs


def setup_inputs(seed=0):
    import zlib

    import numpy as np

    out = dict(_drawn_inputs(seed))
    spreads = {}
    factors = {'sinks': 3.831, 'g_post': 3.816}
    for name, (base, spread) in spreads.items():
        noise = np.random.default_rng([zlib.crc32(name.encode()), seed]).standard_normal(out[name].shape)
        drawn = base * np.exp(spread * noise) if base else spread * noise
        out[name] = __import__('jax').numpy.asarray(drawn.astype(out[name].dtype))
    for name, factor in factors.items():
        out[name] = (out[name] * factor).astype(out[name].dtype)
    return out
```

```python
from contextlib import ExitStack

import concourse.bass as bass
from concourse import mybir

F32 = mybir.dt.float32
F32R = mybir.dt.float32r
BF16 = mybir.dt.bfloat16
ALU = mybir.AluOpType
ACT = mybir.ActivationFunctionType

P = 128
SEQ = 2048
DM = 1024
KT = DM // P
SEC = 512
HALF = 1024
HEADS = 4
CHUNKS = HALF // P
PER_SEC = SEC // P
TILES = SEQ // P
EPS = 1e-6
NEG = -1e30
KEYS = 2 * P

COL = {"rq": 0, "rk": 512, "rv": 1024, "rg": 1536, "aq": 2048, "ak": 2560, "av": 2688, "ag": 2816}
A_UNITS = [("aq", 0), ("rg", 0), ("ag", 0), ("aq", 1), ("rg", 1), ("ag", 1)]
B_UNITS = [("rk", 0), ("rv", 0), ("rq", 0), ("rk", 1), ("rv", 1), ("rq", 1)]
K_UNITS = [("ak", 0), ("av", 0), ("ak", 1), ("av", 1)]
GROUPS = {"A": ["aq", "rg", "ag"], "B": ["rk", "rv", "rq"], "K": ["ak", "av"]}
HALF_GROUPS = 3 + 2 + 6 * HEADS - 3
HALF_UNITS = 2 * HALF_GROUPS
IN_GROUPS = 2 * HALF_GROUPS
OUT_CHUNKS = DM // P

C_MASK, C_DIST, C_HEAD, N_HEAD = 0, P, P + KEYS, 8
C_ALL = C_HEAD + HEADS * N_HEAD
H_SLOPE, H_GCINV, H_GC, H_XI2, H_XIH, H_ZETA = 0, 2, 3, 4, 5, 6


def wait_apart(eng, sem, count):
    if not isinstance(count, int):
        eng.wait_ge(sem, 1)
    eng.wait_ge(sem, count)


class Phase:

    def __init__(self, kind, t, j):
        self.kind, self.t, self.j = kind, t, j
        self.p = 4 * t + j
        self.groups = GROUPS[kind]
        self.n = len(self.groups)
        first = isinstance(j, int) and j == 0 and kind == "B"
        base = {"A": 5, "B": 0 if first else 2, "K": 3}[kind] + HALF_GROUPS * t
        steps = 0 if kind == "K" or first else j
        self.w0, self.w = base, base + 6 * steps
        self.u = 2 * base + 12 * steps

    def slot(self, g):
        return (self.w0 + g) % 3

    def raw(self, g):
        return (self.w0 + g) % 2

    def group_used(self, g):
        return self.u + self.n + g + 1


def nth(p, sec):
    return 2 * p + sec + 1


def hybrid_layer(nc, x, g_pre, w_in, sinks, w_out, g_post, consts, mix, out):
    ctx = ExitStack()
    with ctx:
        def sb(name, shape, dt=F32):
            return ctx.enter_context(nc.sbuf_tensor(name, shape, dt))

        def sem(name):
            return ctx.enter_context(nc.semaphore(name))

        cst = sb("cst", [P, C_ALL])
        ident = sb("ident", [P, P])
        gain = sb("gain", [P, DM])
        sink_all = sb("sink_all", [P, 2, HEADS])
        big = sb("big", [P, 3, 2, KT, SEC], F32R)
        wslot = sb("wslot", [P, 3, 2, KT, P], F32R)
        wraw = sb("wraw", [P, 2, KT, P])
        xt = sb("xt", [P, 2, DM])
        junk = sb("junk", [P, DM], BF16)
        rk_t = sb("rk_t", [P, HALF])
        rv_t = sb("rv_t", [P, HALF])
        rq_t = sb("rq_t", [P, HALF])
        aq_t = sb("aq_t", [P, HALF])
        gate = {"rg": sb("rgate", [P, HALF]), "ag": sb("agate", [P, HALF])}
        k_nat = sb("k_nat", [P, 2, P])
        v_nat = sb("v_nat", [P, 2, P])
        p_ret = sb("p_ret", [P, 2, P])
        state = sb("state", [P, P])
        state_all = sb("state_all", [P, HEADS, P])
        o_ret = sb("o_ret", [P, CHUNKS, P])
        ak_t = sb("ak_t", [P, (CHUNKS + 1) * P])
        av_n = sb("av_n", [P, CHUNKS + 1, P])
        bias = sb("bias", [P, 2, KEYS])
        score = sb("score", [P, 2, 2, KEYS + 1])
        p_t = sb("p_t", [P, 2, 2, P])
        o_att = sb("o_att", [P, P])
        ca = sb("ca", [P, N_HEAD])
        cb = sb("cb", [P, N_HEAD])
        cz = sb("cz", [P, 1])
        sink = sb("sink", [P, 2])
        bn = sb("bn", [P, CHUNKS, 6])
        mv = sb("mv", [P, CHUNKS, 2])
        zvar = sb("zvar", [P, CHUNKS])
        rvar = sb("rvar", [P, CHUNKS])
        rscale = sb("rscale", [P, CHUNKS])
        minus_half = sb("minus_half", [P, PER_SEC])
        top = sb("top", [P, 2, 2])
        ntop = sb("ntop", [P, 2, 2])
        esum = sb("esum", [P, 4, 2])
        rsum = sb("rsum", [P, 4, 2])
        xss = sb("xss", [P, 2, 2])
        xz = sb("xz", [P, 2])
        xr = sb("xr", [P, 2])
        credit = sb("credit", [P, 4])
        ticket = sb("ticket", [P, 1])

        proj = [ctx.enter_context(nc.psum_tensor(f"proj{i}", [P, SEC], F32)) for i in range(2)]
        ps_a, ps_b, ps_c, ps_d, ps_e, ps_f = [
            ctx.enter_context(nc.psum_tensor(f"ps_{i}", [P, SEC], F32)) for i in "abcdef"]

        const_in = sem("const_in")
        gain_in = sem("gain_in")
        ident_made = sem("ident_made")
        halves_made = sem("halves_made")
        x_in = [sem(f"x_in{i}") for i in range(2)]
        x_squared = sem("x_squared")
        x_var = sem("x_var")
        x_rs = sem("x_rs")
        x_normed = sem("x_normed")
        x_turned = sem("x_turned")
        x_hi = sem("x_hi")
        x_lo = sem("x_lo")
        raw_in = [sem(f"raw_in{i}") for i in range(2)]
        wout_in = [sem(f"wout_in{i}") for i in range(2)]
        w_hi = sem("w_hi")
        w_ready = sem("w_ready")
        unit_done = sem("unit_done")
        copied = {k: sem(f"copied_{k}") for k in ("rk", "rv", "rq", "aq", "ak", "av")}
        tanh_done = {k: sem(f"tanh_{k}") for k in ("rg", "ag")}
        gated = {k: sem(f"gated_{k}") for k in ("rg", "ag")}
        v_turned = sem("v_turned")
        v_kept = sem("v_kept")
        ret_consts = sem("ret_consts")
        zeta_here = sem("zeta_here")
        ret_scored = sem("ret_scored")
        kv_copied = sem("kv_copied")
        ret_masked = sem("ret_masked")
        ret_summed = sem("ret_summed")
        o_copied = sem("o_copied")
        state_ready = sem("state_ready")
        state_saved = sem("state_saved")
        bn_done = sem("bn_done")
        aggr_done = sem("aggr_done")
        var_ready = sem("var_ready")
        rvar_ready = sem("rvar_ready")
        scale_ready = sem("scale_ready")
        o_normed = sem("o_normed")
        ret_turned = sem("ret_turned")
        combined = {k: sem(f"combined_{k}") for k in ("rg", "ag")}
        stored = {k: [sem(f"stored_{k}{i}") for i in range(2)] for k in ("rg", "ag")}
        att_consts = sem("att_consts")
        bias_made = sem("bias_made")
        att_scored = sem("att_scored")
        att_biased = sem("att_biased")
        max_ready = sem("max_ready")
        exp_done = sem("exp_done")
        p_turned = sem("p_turned")
        p_copied = sem("p_copied")
        rsum_ready = sem("rsum_ready")
        att_summed = sem("att_summed")
        oatt_scaled = sem("oatt_scaled")
        att_turned = sem("att_turned")
        mix_in = [sem(f"mix_in{i}") for i in range(2)]
        mix_hi = sem("mix_hi")
        mix_ready = sem("mix_ready")
        res_in = [sem(f"res_in{i}") for i in range(2)]
        out_done = sem("out_done")
        out_copied = sem("out_copied")
        out_ms = sem("out_ms")
        out_var = sem("out_var")
        out_rs = sem("out_rs")
        out_scaled = sem("out_scaled")
        out_added = sem("out_added")
        out_stored = [sem(f"out_stored{i}") for i in range(2)]

        w_in_v = w_in.rearrange("(k p) c -> p k c", p=P)
        w_out_v = w_out.rearrange("(k p) c -> p k c", p=P)
        w_out_pair = w_out[4 * P:, :].rearrange("(h k q) c -> h q k c", h=2, k=HEADS)
        n_tok = {"rg": 0, "ag": HEADS}

        def hbuf(t, sec):
            return (2 * t + sec) % 3

        mix_raw = [rk_t[:, :], rv_t[:, :]]
        out_sb = [rq_t[:, :], o_ret[:, :, :].rearrange("p c d -> p (c d)")]

        def mix_split(i, part):
            return big[:, 2, part, :, 2 * P * (i % 2):2 * P * (i % 2) + P]

        def w_out_at(c):
            return 1 if c == 0 else 0

        block = ctx.enter_context(nc.Block())

        @block.sync
        def _(sp):
            def load_w(ph, g):
                kind, j, b = ph.groups[g], ph.j, ph.raw(g)
                if not (isinstance(ph.w, int) and ph.w + g < 2):
                    sp.wait_ge(w_ready, ph.w + g - 1)
                dst = wraw[:, b, :, :]
                if kind in ("aq", "ag"):
                    for h in range(2):
                        src = w_in_v[:, :, bass.ds(COL[kind] + 256 * h + 64 * j, 64)]
                        sp.dma_start(dst[:, :, 64 * h:64 * h + 64], src).then_inc(raw_in[b], 16)
                else:
                    col = COL[kind] if kind in ("ak", "av") else COL[kind] + P * j
                    for h in (1, 0):
                        src = w_in_v[:, 4 * h:4 * h + 4, bass.ds(col, P)]
                        sp.dma_start(dst[:, 4 * h:4 * h + 4, :], src).then_inc(raw_in[b], 16)

            def load_x(i):
                if i >= 2:
                    sp.wait_ge(x_turned, i - 1)
                sp.dma_start(xt[:, i % 2, :], x[i * P:(i + 1) * P, :]).then_inc(x_in[i % 2], 16)

            def store(kind, t, j, sec):
                sp.wait_ge(combined[kind], nth(4 * t + j, sec))
                tile = PER_SEC * (2 * t + sec)
                dst = mix[tile:tile + PER_SEC, :, bass.ds(n_tok[kind] + j, 1), :]
                sp.dma_start(dst.rearrange("i p g n -> p (i g) n"),
                             gate[kind][:, SEC * sec:SEC * (sec + 1)].rearrange("p (i n) -> p i n", n=P)
                             ).then_inc(stored[kind][sec], 16)

            def load_w_out(q):
                b = (IN_GROUPS + q) % 2
                sp.wait_ge(w_ready, IN_GROUPS + q - 1)
                cols = slice(q * P, (q + 1) * P)
                sp.dma_start(wraw[:, b, 0:4, :], w_out_v[:, 0:4, cols]).then_inc(wout_in[b], 16)
                for h in range(2):
                    sp.dma_start(wraw[64 * h:64 * h + 64, b, 4:8, :],
                                 w_out_pair[h, :, :, cols]).then_inc(wout_in[b], 16)

            first = Phase("B", 0, 0)
            load_x(0)
            sp.dma_start(gain[:, :], g_pre.partition_broadcast(P)).then_inc(gain_in, 16)
            load_x(1)
            sp.dma_start(cst[:, :], consts).then_inc(const_in, 16)
            sp.dma_start(sink_all[:, :, :].rearrange("p a b -> p (a b)"),
                         sinks.partition_broadcast(P)).then_inc(const_in, 16)
            load_w(first, 0)
            load_w(first, 1)
            load_x(2)
            load_x(3)
            load_w(first, 2)
            for i in range(4, 8):
                load_x(i)
            for t in range(2):
                nxt = Phase("K", t, 0)
                load_w(nxt, 0)
                load_w(nxt, 1)
                if t == 1:
                    store("ag", 0, 3, 0)
                    store("ag", 0, 3, 1)
                nxt = Phase("A", t, 0)
                for g in range(3):
                    load_w(nxt, g)
                with sp.Fori(0, HEADS - 1) as j:
                    nxt = Phase("B", t, j + 1)
                    load_w(nxt, 0)
                    load_w(nxt, 1)
                    store("rg", t, j, 0)
                    load_w(nxt, 2)
                    store("rg", t, j, 1)
                    nxt = Phase("A", t, j + 1)
                    load_w(nxt, 0)
                    load_w(nxt, 1)
                    store("ag", t, j, 0)
                    load_w(nxt, 2)
                    store("ag", t, j, 1)
                if t == 0:
                    nxt = Phase("B", 1, 0)
                    for i in range(8, 12):
                        load_x(i)
                    load_w(nxt, 0)
                    load_w(nxt, 1)
                    for i in range(12, 16):
                        load_x(i)
                    store("rg", 0, 3, 0)
                    load_w(nxt, 2)
                    store("rg", 0, 3, 1)

            def load_mix(i):
                if i >= 2:
                    sp.wait_ge(mix_ready, i - 1)
                else:
                    sp.wait_ge(ret_summed, 8 * CHUNKS)
                sp.dma_start(mix_raw[i % 2].rearrange("p (g n) -> p g n", n=P),
                             mix[i, :, :, :]).then_inc(mix_in[i % 2], 16)
                if i >= 2:
                    sp.wait_ge(out_added, i - 1)
                else:
                    sp.wait_ge(x_turned, TILES)
                sp.dma_start(xt[:, i % 2, :], x[i * P:(i + 1) * P, :]).then_inc(res_in[i % 2], 16)

            def store_out(i):
                sp.wait_ge(out_added, i + 1)
                sp.dma_start(out[i * P:(i + 1) * P, :], out_sb[i % 2]).then_inc(out_stored[i % 2], 16)

            sp.wait_ge(x_normed, TILES)
            sp.dma_start(gain[:, :], g_post.partition_broadcast(P)).then_inc(gain_in, 16)
            for q in range(4):
                load_w_out(q)
            store("rg", 1, 3, 0)
            load_w_out(4)
            load_w_out(5)
            store("rg", 1, 3, 1)
            for sec in range(2):
                for k in ("rg", "ag"):
                    sp.wait_ge(stored[k][sec], 16 * (HEADS + 1))
            load_mix(0)
            load_mix(1)
            load_w_out(6)
            load_w_out(7)
            store("ag", 1, 3, 0)
            load_mix(2)
            store("ag", 1, 3, 1)
            load_mix(3)
            for i in range(TILES):
                if i >= 2 and i + 2 < TILES:
                    if i + 2 == TILES // 2:
                        for sec in range(2):
                            for k in ("rg", "ag"):
                                sp.wait_ge(stored[k][sec], 16 * (2 * HEADS + 1))
                    load_mix(i + 2)
                store_out(i)
            for i in range(2):
                sp.wait_ge(out_stored[i], 16 * TILES // 2)

        @block.gpsimd
        def _(pool):
            nc.gpsimd.memset(minus_half[:, :], -0.5).then_inc(halves_made, 1)
            nc.gpsimd.memset(ident[:, :], 0.0).then_inc(ident_made, 1)
            pool.wait_ge(ident_made, 1)
            nc.gpsimd.affine_select(out=ident[:, :], in_=ident[:, :], compare_op=ALU.not_equal, fill=1.0,
                                    base=0, pattern=[[-1, P]], channel_multiplier=1).then_inc(ident_made, 1)

            def split_group(ph, g, used):
                s, b = ph.slot(g), ph.raw(g)
                pool.wait_ge(raw_in[b], 32 * ((ph.w0 + g) // 2 + 1) + 16 * (ph.w - ph.w0))
                if used is not None:
                    pool.wait_ge(unit_done, used)
                nc.gpsimd.tensor_tensor(ticket[:, :], minus_half[:, 0:1], minus_half[:, 0:1], ALU.mult)
                nc.gpsimd.tensor_copy(wslot[:, s, 0, :, :], wraw[:, b, :, :]).then_inc(w_hi, 1)
                pool.wait_ge(w_hi, ph.w + g + 1)
                nc.gpsimd.tensor_tensor(wslot[:, s, 1, :, :], wraw[:, b, :, :], wslot[:, s, 0, :, :],
                                        ALU.subtract).then_inc(w_ready, 1)

            def x_power(i):
                pool.wait_ge(x_var, i + 1)
                nc.gpsimd.tensor_tensor(xr[:, i % 2:i % 2 + 1], xz[:, i % 2:i % 2 + 1],
                                        minus_half[:, 0:1], ALU.pow).then_inc(x_rs, 1)

            def ret_power(p, sec):
                pool.wait_ge(var_ready, nth(p, sec))
                cs = slice(PER_SEC * sec, PER_SEC * (sec + 1))
                nc.gpsimd.tensor_tensor(rvar[:, cs], zvar[:, cs], minus_half[:, :],
                                        ALU.pow).then_inc(rvar_ready, 1)

            pool.wait_ge(halves_made, 1)
            first = Phase("B", 0, 0)
            x_power(0)
            x_power(1)
            split_group(first, 0, None)
            x_power(2)
            split_group(first, 1, None)
            x_power(3)
            split_group(first, 2, None)
            for i in range(4, 8):
                x_power(i)
            for t in range(2):
                cur, nxt = Phase("B", t, 0), Phase("K", t, 0)
                for g in range(2):
                    split_group(nxt, g, cur.group_used(g))
                cur, nxt = nxt, Phase("A", t, 0)
                split_group(nxt, 0, cur.u)
                split_group(nxt, 1, cur.group_used(0))
                split_group(nxt, 2, cur.group_used(1))
                with pool.Fori(0, HEADS - 1) as j:
                    cur, nxt = Phase("A", t, j), Phase("B", t, j + 1)
                    ret_power(cur.p, 0)
                    split_group(nxt, 0, cur.group_used(0))
                    ret_power(cur.p, 1)
                    split_group(nxt, 1, cur.group_used(1))
                    split_group(nxt, 2, cur.group_used(2))
                    cur, nxt = nxt, Phase("A", t, j + 1)
                    for g in range(3):
                        split_group(nxt, g, cur.group_used(g))
                if t == 0:
                    cur, nxt = Phase("A", 0, 3), Phase("B", 1, 0)
                    for i in range(8, 13):
                        x_power(i)
                    ret_power(3, 0)
                    x_power(13)
                    x_power(14)
                    x_power(15)
                    split_group(nxt, 0, cur.group_used(0))
                    ret_power(3, 1)
                    split_group(nxt, 1, cur.group_used(1))
                    split_group(nxt, 2, cur.group_used(2))

            def split_w_out(q):
                b, w, c = (IN_GROUPS + q) % 2, IN_GROUPS + q, q // 4
                cols = slice(P * (q % 4), P * (q % 4) + P)
                pool.wait_ge(wout_in[b], 48 * (q // 2 + 1))
                if c == 1:
                    pool.wait_ge(unit_done, 2 * HALF_UNITS)
                nc.gpsimd.tensor_copy(big[:, w_out_at(c), 0, :, cols], wraw[:, b, :, :]).then_inc(w_hi, 1)
                pool.wait_ge(w_hi, w + 1)
                nc.gpsimd.tensor_tensor(big[:, w_out_at(c), 1, :, cols], wraw[:, b, :, :],
                                        big[:, w_out_at(c), 0, :, cols], ALU.subtract).then_inc(w_ready, 1)

            def split_mix(i):
                pool.wait_ge(mix_in[i % 2], 16 * (i // 2 + 1))
                if i >= 2:
                    pool.wait_ge(out_done, 2 * (i - 2) + 2)
                else:
                    pool.wait_ge(unit_done, 2 * HALF_UNITS - 3)
                raw = mix_raw[i % 2].rearrange("p (g n) -> p g n", n=P)
                nc.gpsimd.tensor_copy(mix_split(i, 0), raw).then_inc(mix_hi, 1)
                pool.wait_ge(mix_hi, i + 1)
                nc.gpsimd.tensor_tensor(mix_split(i, 1), raw, mix_split(i, 0),
                                        ALU.subtract).then_inc(mix_ready, 1)

            def out_power(i):
                pool.wait_ge(out_var, i + 1)
                nc.gpsimd.tensor_tensor(xr[:, i % 2:i % 2 + 1], xz[:, i % 2:i % 2 + 1],
                                        minus_half[:, 0:1], ALU.pow).then_inc(out_rs, 1)

            for q in range(4):
                split_w_out(q)
            ret_power(7, 0)
            ret_power(7, 1)
            split_mix(0)
            split_mix(1)
            for q in range(4, 8):
                split_w_out(q)
            for i in range(TILES):
                out_power(i)
                if i + 2 < TILES:
                    split_mix(i + 2)

        @block.tensor
        def _(pe):
            def turn_x(i):
                pe.wait_ge(x_normed, i + 1)
                if i >= 1:
                    pe.wait_ge(x_lo, 2 * i)
                for k in range(KT):
                    bank = ps_e if k < 4 else ps_f
                    last = nc.tensor.transpose(bank[:, P * (k % 4):P * (k % 4) + P],
                                               xt[:, i % 2, P * k:P * (k + 1)], ident[:, :])
                last.then_inc(x_turned, 1)

            def unit_half(ph, units, s, bank_free):
                u, half = divmod(s, 2)
                kind, sec = units[u]
                g = ph.groups.index(kind)
                if half == 0:
                    if bank_free is not None:
                        pe.wait_ge(*bank_free)
                    if sec == 0:
                        pe.wait_ge(w_ready, ph.w + g + 1)
                w, h = ph.slot(g), hbuf(ph.t, sec)
                bank = proj[u % 2]
                for k in range(4 * half, 4 * half + 4):
                    for wp, hp in ((0, 0), (0, 1), (1, 0)):
                        last = nc.tensor.matmul(bank[:, :], wslot[:, w, wp, k, :], big[:, h, hp, k, :],
                                                start=(k == 0 and wp + hp == 0), stop=(k == KT - 1 and wp == 1))
                if half == 1:
                    last.then_inc(unit_done, 1)

            def evacuated(kind, sec, p):
                return (gated if kind in gated else copied)[kind], nth(p, sec)

            def ret_score(p, c):
                sec, par = c // PER_SEC, slice(c * P, (c + 1) * P)
                if c % PER_SEC == 0:
                    for k in ("rk", "rv", "rq"):
                        pe.wait_ge(copied[k], nth(p, sec))
                nc.tensor.transpose(ps_a[:, 0:P], rk_t[:, par], ident[:, :])
                nc.tensor.transpose(ps_a[:, P:2 * P], rv_t[:, par], ident[:, :])
                nc.tensor.matmul(ps_b[:, 0:P], rk_t[:, par], rq_t[:, par],
                                 start=True, stop=True).then_inc(ret_scored, 1)

            def ret_sum(p, c):
                n = CHUNKS * p + c
                pe.wait_ge(kv_copied, n + 1)
                pe.wait_ge(ret_masked, n + 1)
                pe.wait_ge(state_ready, (CHUNKS + 1) * p + c + 1)
                nc.tensor.matmul(ps_c[:, P:2 * P], k_nat[:, c % 2, :], v_nat[:, c % 2, :], start=True, stop=True)
                nc.tensor.matmul(ps_c[:, 0:P], p_ret[:, c % 2, :], v_nat[:, c % 2, :], start=True, stop=False)
                nc.tensor.matmul(ps_c[:, 0:P], rq_t[:, c * P:(c + 1) * P], state[:, :],
                                 start=False, stop=True).then_inc(ret_summed, 1)

            def ret_turn(p, sec):
                pe.wait_ge(o_normed, nth(p, sec))
                for c in range(PER_SEC):
                    last = nc.tensor.transpose(ps_d[:, c * P:(c + 1) * P], o_ret[:, PER_SEC * sec + c, :],
                                               ident[:, :])
                last.then_inc(ret_turned, 1)

            def att_score(p, t, b):
                if b % PER_SEC == 0:
                    pe.wait_ge(copied["aq"], nth(p, b // PER_SEC))
                    pe.wait_ge(copied["ak"], nth(t, 1))
                if b >= 1:
                    pe.wait_ge(att_biased, CHUNKS * p + b)
                lo = P if t == 0 and b == 0 else 0
                for h, bank in ((0, ps_a), (1, ps_b)):
                    rows = slice(64 * h, 64 * h + 64)
                    last = nc.tensor.matmul(bank[:, lo:KEYS], aq_t[rows, b * P:(b + 1) * P],
                                            ak_t[rows, b * P + lo:b * P + KEYS], start=True, stop=True)
                last.then_inc(att_scored, 1)

            def att_turn_p(p, t, b):
                pe.wait_ge(exp_done, CHUNKS * p + b + 1)
                for h in range(2):
                    for e in range(1 if t == 0 and b == 0 else 0, 2):
                        at = P * (2 * h + e)
                        last = nc.tensor.transpose(ps_c[:, at:at + P], score[:, b % 2, h, P * e:P * (e + 1)],
                                                   ident[:, :])
                last.then_inc(p_turned, 1)

            def att_sum(p, t, b):
                pe.wait_ge(p_copied, CHUNKS * p + b + 1)
                if b == 0:
                    pe.wait_ge(v_kept, nth(t, 1))
                es = (1,) if t == 0 and b == 0 else (0, 1)
                for h in range(2):
                    for e in es:
                        last = nc.tensor.matmul(ps_e[:, 64 * h:64 * h + 64], p_t[:, h, e, :],
                                                av_n[:, b + e, 64 * h:64 * h + 64],
                                                start=(e == es[0]), stop=(e == 1))
                last.then_inc(att_summed, 1)

            def att_turn_o(p, b):
                pe.wait_ge(oatt_scaled, CHUNKS * p + b + 1)
                if b % PER_SEC == 0:
                    if b == 0:
                        pe.wait_ge(combined["rg"], nth(p, 1))
                    else:
                        pe.wait_ge(combined["ag"], nth(p, 0))
                nc.tensor.transpose(ps_d[:, P * (b % PER_SEC):P * (b % PER_SEC) + P], o_att[:, :],
                                    ident[:, :]).then_inc(att_turned, 1)

            def att_steps(p, t, s):
                if 0 <= s - 4 < CHUNKS:
                    att_turn_o(p, s - 4)
                if 0 <= s - 3 < CHUNKS:
                    att_sum(p, t, s - 3)
                if 0 <= s - 2 < CHUNKS:
                    att_turn_p(p, t, s - 2)
                if s < CHUNKS:
                    att_score(p, t, s)

            def phase_a(t, j, x_tiles):
                ph = Phase("A", t, j)
                for s in range(12):
                    if s == 7:
                        ret_turn(ph.p, 0)
                    if 0 <= s - 1 < CHUNKS:
                        ret_sum(ph.p, s - 1)
                    if s < CHUNKS:
                        ret_score(ph.p, s)
                    if s == 11:
                        pe.wait_ge(combined["rg"], nth(ph.p, 0))
                        ret_turn(ph.p, 1)
                    if s in x_tiles:
                        turn_x(x_tiles[s])
                    u = s // 2
                    if u >= 2:
                        free = evacuated(*A_UNITS[u - 2], ph.p)
                    else:
                        free = evacuated(*B_UNITS[4 + u], ph.p)
                    unit_half(ph, A_UNITS, s, free)

            def phase_b(t, j, att_t, att_p):
                ph = Phase("B", t, j)
                for s in range(12):
                    if att_p is not None:
                        att_steps(att_p, att_t, s)
                    elif s < 4:
                        turn_x(4 + s)
                    u = s // 2
                    if s in (0, 6) and isinstance(j, int) and j == 0:
                        pe.wait_ge(x_lo, 2 * PER_SEC * (2 * t + s // 6 + 1))
                    if u >= 2:
                        free = evacuated(*B_UNITS[u - 2], ph.p)
                    elif att_p is not None:
                        free = evacuated(*A_UNITS[4 + u], att_p)
                    else:
                        free = None
                    unit_half(ph, B_UNITS, s, free)

            def turn_v(t, sec):
                pe.wait_ge(copied["av"], nth(t, sec))
                if sec == 1:
                    pe.wait_ge(v_kept, nth(t, 0))
                for b in range(PER_SEC):
                    at = SEC * sec + P * b
                    last = nc.tensor.transpose(ps_f[:, P * b:P * (b + 1)], aq_t[:, at:at + P], ident[:, :])
                last.then_inc(v_turned, 1)

            def phase_k(t):
                ph = Phase("K", t, 0)
                for s in range(8):
                    if s == 5:
                        turn_v(t, 0)
                    u = s // 2
                    free = evacuated(*K_UNITS[u - 2], t) if u >= 2 else evacuated(*B_UNITS[4 + u], ph.p)
                    unit_half(ph, K_UNITS, s, free)
                pe.wait_ge(copied["ak"], nth(t, 1))
                turn_v(t, 1)

            pe.wait_ge(ident_made, 2)
            for i in range(4):
                turn_x(i)
            for t in range(2):
                phase_b(t, 0, 0, None if t == 0 else 3)
                phase_k(t)
                with pe.Fori(0, HEADS - 1) as j:
                    phase_a(t, j, {})
                    phase_b(t, j + 1, t, 4 * t + j)
                phase_a(t, 3, {1: 8, 2: 9, 3: 10, 4: 11, 6: 12, 7: 13, 8: 14, 9: 15} if t == 0 else {})

            def out_quarter(i, q):
                c, half = divmod(q, 2)
                if q == 0:
                    pe.wait_ge(mix_ready, i + 1)
                if half == 0:
                    if i == 0:
                        pe.wait_ge(*evacuated(*A_UNITS[4 + c], 7))
                        pe.wait_ge(w_ready, IN_GROUPS + 4 * (c + 1))
                    else:
                        pe.wait_ge(out_copied, 2 * (i - 1) + c + 1)
                for k in range(4 * half, 4 * half + 4):
                    for mp, wp in ((0, 0), (0, 1), (1, 0)):
                        last = nc.tensor.matmul(proj[c][:, :], mix_split(i, mp)[:, k, :],
                                                big[:, w_out_at(c), wp, k, :],
                                                start=(k == 0 and mp + wp == 0), stop=(k == KT - 1 and mp == 1))
                if half == 1:
                    last.then_inc(out_done, 1)

            for i in range(TILES):
                for q in range(4):
                    if 4 * i + q < 12:
                        att_steps(7, 1, 4 * i + q)
                    out_quarter(i, q)

        @block.scalar
        def _(act):
            def x_square(i):
                act.wait_ge(x_in[i % 2], 16 * (i // 2 + 1))
                if i >= 2:
                    act.wait_ge(x_var, i - 1)
                if i >= 1:
                    act.wait_ge(x_squared, i)
                nc.scalar.activation(junk[:, :], xt[:, i % 2, :], ACT.Square,
                                     accum_out=xss[:, i % 2, 0:1]).then_inc(x_squared, 1)

            def x_high(i):
                b, at = (i // PER_SEC) % 3, P * (i % PER_SEC)
                act.wait_ge(x_turned, i + 1)
                if i == 12:
                    act.wait_ge(unit_done, Phase("A", 0, 3).u + 3)
                for h, bank in ((0, ps_e), (1, ps_f)):
                    nc.scalar.copy(big[:, b, 0, 4 * h:4 * h + 4, at:at + P],
                                   bank[:, :].rearrange("p (k n) -> p k n", n=P)).then_inc(x_hi, 1)

            def evacuate(ph, units, u):
                kind, sec = units[u]
                bank, cols = proj[u % 2], slice(SEC * sec, SEC * (sec + 1))
                act.wait_ge(unit_done, ph.u + u + 1)
                if kind in ("rg", "ag"):
                    act.wait_ge(stored[kind][sec], 16 * ph.p + 16)
                    nc.scalar.activation(gate[kind][:, cols], bank[:, :], ACT.Tanh,
                                         scale=0.5).then_inc(tanh_done[kind], 1)
                    return
                dst = {"rk": rk_t, "rv": rv_t, "rq": rq_t, "aq": aq_t, "av": aq_t, "ak": ak_t}[kind]
                if kind == "ak":
                    cols = slice(P + SEC * sec, P + SEC * (sec + 1))
                if kind == "aq":
                    nc.scalar.activation(dst[:, cols], bank[:, :], ACT.Copy,
                                         scale=0.125).then_inc(copied[kind], 1)
                else:
                    nc.scalar.copy(dst[:, cols], bank[:, :]).then_inc(copied[kind], 1)

            def ret_copies(p, c):
                act.wait_ge(ret_scored, CHUNKS * p + c + 1)
                nc.scalar.copy(k_nat[:, c % 2, :], ps_a[:, 0:P])
                nc.scalar.activation(v_nat[:, c % 2, :], ps_a[:, P:2 * P], ACT.Copy,
                                     scale=cz[:, 0:1]).then_inc(kv_copied, 1)

            def att_exp(p, t, b):
                act.wait_ge(max_ready, CHUNKS * p + b + 1)
                lo = P if t == 0 and b == 0 else 0
                for h in range(2):
                    s = score[:, b % 2, h, lo:KEYS + 1]
                    last = nc.scalar.activation(s, s, ACT.Exp, bias=ntop[:, b % 2, h:h + 1],
                                                accum_out=esum[:, b % 4, h:h + 1])
                last.then_inc(exp_done, 1)

            def att_copy_p(p, t, b):
                act.wait_ge(p_turned, CHUNKS * p + b + 1)
                lo = 1 if t == 0 and b == 0 else 0
                nc.scalar.copy(p_t[:, :, lo:2, :],
                               ps_c[:, :].rearrange("p (h e n) -> p h e n", h=2, e=2)[:, :, lo:2, :]
                               ).then_inc(p_copied, 1)

            def att_steps(p, t, s):
                if 0 <= s - 2 < CHUNKS:
                    att_copy_p(p, t, s - 2)
                if s < CHUNKS:
                    att_exp(p, t, s)

            def phase_a(t, j, x_pre, x_main):
                ph = Phase("A", t, j)
                nc.scalar.copy(cz[:, 0:1], cst[:, bass.ds(C_HEAD + H_ZETA + N_HEAD * j, 1)]).then_inc(zeta_here, 1)
                for s in range(12):
                    if s >= 2 and s % 2 == 0:
                        evacuate(ph, A_UNITS, s // 2 - 1)
                    if s < CHUNKS:
                        if s == 0:
                            act.wait_ge(zeta_here, ph.p + 1)
                        ret_copies(ph.p, s)
                    if s in x_main:
                        x_high(x_main[s])
                    for i in x_pre.get(s, ()):
                        x_square(i)
                evacuate(ph, A_UNITS, 5)

            def phase_b(t, j, att_t, att_p):
                ph = Phase("B", t, j)
                for s in range(12):
                    if s >= 2 and s % 2 == 0:
                        evacuate(ph, B_UNITS, s // 2 - 1)
                    if att_p is not None:
                        att_steps(att_p, att_t, s)
                    elif s < 4:
                        x_high(4 + s)
                        if 6 + s < 8:
                            x_square(6 + s)
                evacuate(ph, B_UNITS, 5)

            def keep_v(t, sec):
                act.wait_ge(v_turned, nth(t, sec))
                nc.scalar.copy(av_n[:, 1 + PER_SEC * sec:1 + PER_SEC * (sec + 1), :],
                               ps_f[:, :].rearrange("p (b n) -> p b n", n=P)).then_inc(v_kept, 1)

            def phase_k(t):
                ph = Phase("K", t, 0)
                if t == 1:
                    act.wait_ge(att_summed, 4 * CHUNKS)
                    nc.scalar.copy(ak_t[:, 0:P], ak_t[:, CHUNKS * P:(CHUNKS + 1) * P])
                    nc.scalar.copy(av_n[:, 0, :], av_n[:, CHUNKS, :])
                evacuate(ph, K_UNITS, 0)
                evacuate(ph, K_UNITS, 1)
                keep_v(t, 0)
                evacuate(ph, K_UNITS, 2)
                evacuate(ph, K_UNITS, 3)
                keep_v(t, 1)

            act.wait_ge(const_in, 32)
            x_square(0)
            x_square(1)
            for i in range(4):
                x_high(i)
                x_square(i + 2)
            for t in range(2):
                phase_b(t, 0, 0, None if t == 0 else 3)
                phase_k(t)
                with act.Fori(0, HEADS - 1) as j:
                    phase_a(t, j, {}, {})
                    phase_b(t, j + 1, t, 4 * t + j)
                if t == 0:
                    phase_a(0, 3, {0: (8, 9), 1: (10,), 2: (11,), 3: (12,), 4: (13,), 6: (14,), 7: (15,)},
                            {1: 8, 2: 9, 3: 10, 4: 11, 6: 12, 7: 13, 8: 14, 9: 15})
                else:
                    phase_a(1, 3, {}, {})

            def out_copy(i, c):
                act.wait_ge(out_done, 2 * i + c + 1)
                if i >= 2 and c == 0:
                    act.wait_ge(out_stored[i % 2], 16 * (i // 2))
                    act.wait_ge(out_ms, i - 1)
                if 2 * i + c >= 1:
                    act.wait_ge(out_copied, 2 * i + c)
                else:
                    act.wait_ge(x_squared, TILES)
                nc.scalar.copy(out_sb[i % 2][:, SEC * c:SEC * (c + 1)], proj[c][:, :])
                nc.scalar.activation(junk[:, 0:SEC], proj[c][:, :], ACT.Square,
                                     accum_out=xss[:, i % 2, c:c + 1]).then_inc(out_copied, 1)

            for i in range(TILES):
                for q in range(4):
                    s = 4 * i + q
                    if q == 2:
                        out_copy(i, 0)
                    if q == 0 and i >= 1:
                        out_copy(i - 1, 1)
                    if s < 12:
                        att_steps(7, 1, s)
            out_copy(TILES - 1, 1)

        @block.vector
        def _(dve):
            for i, (k, sec) in enumerate((k, sec) for k in ("rg", "ag") for sec in range(2)):
                nc.vector.memset(credit[:, i:i + 1], 0.0).then_inc(stored[k][sec], 16)

            def x_norm(i):
                b = i % 2
                dve.wait_ge(x_squared, i + 1)
                if i >= 2:
                    dve.wait_ge(x_rs, i - 1)
                nc.vector.tensor_scalar(xz[:, b:b + 1], xss[:, b, 0:1], 1.0 / DM, EPS, ALU.mult,
                                        ALU.add).then_inc(x_var, 1)
                dve.wait_ge(x_rs, i + 1)
                nc.vector.scalar_tensor_tensor(out=xt[:, b, :], in0=xt[:, b, :], scalar=xr[:, b:b + 1],
                                               in1=gain[:, :], op0=ALU.mult, op1=ALU.mult).then_inc(x_normed, 1)

            def x_low(i):
                b, at = (i // PER_SEC) % 3, P * (i % PER_SEC)
                for h, bank in ((0, ps_e), (1, ps_f)):
                    ks = slice(4 * h, 4 * h + 4)
                    dve.wait_ge(x_hi, 2 * i + h + 1)
                    nc.vector.tensor_tensor(big[:, b, 1, ks, at:at + P],
                                            bank[:, :].rearrange("p (k n) -> p k n", n=P),
                                            big[:, b, 0, ks, at:at + P], ALU.subtract).then_inc(x_lo, 1)

            def make_gate(kind, p, sec):
                g = gate[kind][:, SEC * sec:SEC * (sec + 1)]
                bank = proj[A_UNITS.index((kind, sec)) % 2]
                dve.wait_ge(tanh_done[kind], nth(p, sec))
                nc.vector.scalar_tensor_tensor(out=g, in0=g, scalar=1.0, in1=bank[:, :], op0=ALU.add,
                                               op1=ALU.mult).then_inc(gated[kind], 1)

            def combine(kind, p, sec):
                g = gate[kind][:, SEC * sec:SEC * (sec + 1)]
                if kind == "rg":
                    dve.wait_ge(ret_turned, nth(p, sec))
                else:
                    dve.wait_ge(att_turned, CHUNKS * p + PER_SEC * (sec + 1))
                dve.wait_ge(gated[kind], nth(p, sec))
                nc.vector.tensor_tensor(g, ps_d[:, :], g, ALU.mult).then_inc(combined[kind], 1)

            def load_state(t, j, p):
                if t == 0:
                    nc.vector.memset(state[:, :], 0.0).then_inc(state_ready, 1)
                else:
                    dve.wait_ge(state_saved, HEADS)
                    nc.vector.tensor_copy(state[:, :], state_all[:, bass.ds(j, 1), :]).then_inc(state_ready, 1)

            def ret_mask(p, c):
                dve.wait_ge(ret_scored, CHUNKS * p + c + 1)
                nc.vector.scalar_tensor_tensor(out=p_ret[:, c % 2, :], in0=ps_b[:, 0:P],
                                               scalar=ca[:, H_GCINV:H_GCINV + 1], in1=cst[:, C_MASK:C_MASK + P],
                                               op0=ALU.mult, op1=ALU.mult).then_inc(ret_masked, 1)

            def ret_state(p, c):
                dve.wait_ge(ret_summed, CHUNKS * p + c + 1)
                nc.vector.tensor_copy(o_ret[:, c, :], ps_c[:, 0:P]).then_inc(o_copied, 1)
                dve.wait_ge(state_ready, (CHUNKS + 1) * p + c + 1)
                nc.vector.scalar_tensor_tensor(out=state[:, :], in0=state[:, :], scalar=ca[:, H_GC:H_GC + 1],
                                               in1=ps_c[:, P:2 * P], op0=ALU.mult,
                                               op1=ALU.add).then_inc(state_ready, 1)

            def ret_stats(p, c):
                dve.wait_ge(o_copied, CHUNKS * p + c + 1)
                nc.vector.bn_stats(bn[:, c, :], o_ret[:, c, :]).then_inc(bn_done, 1)
                wait_apart(dve, bn_done, CHUNKS * p + c + 1)
                nc.vector.bn_aggr(mv[:, c, :], bn[:, c, :]).then_inc(aggr_done, 1)

            def ret_var(p, sec):
                cs = slice(PER_SEC * sec, PER_SEC * (sec + 1))
                dve.wait_ge(aggr_done, CHUNKS * p + PER_SEC * (sec + 1))
                nc.vector.tensor_scalar(zvar[:, cs], mv[:, cs, 1], ca[:, H_XI2:H_XI2 + 1], EPS, ALU.mult,
                                        ALU.add).then_inc(var_ready, 1)

            def ret_norm(p, sec):
                cs = slice(PER_SEC * sec, PER_SEC * (sec + 1))
                dve.wait_ge(rvar_ready, nth(p, sec))
                nc.vector.tensor_scalar(rscale[:, cs], rvar[:, cs], ca[:, H_XIH:H_XIH + 1], None,
                                        ALU.mult).then_inc(scale_ready, 1)
                dve.wait_ge(scale_ready, nth(p, sec))
                for c in range(PER_SEC * sec, PER_SEC * (sec + 1)):
                    last = nc.vector.tensor_scalar(o_ret[:, c, :], o_ret[:, c, :], mv[:, c, 0:1],
                                                   rscale[:, c:c + 1], ALU.subtract, ALU.mult)
                last.then_inc(o_normed, 1)

            def att_bias(p, t, b):
                dve.wait_ge(att_scored, CHUNKS * p + b + 1)
                lo = P if t == 0 and b == 0 else 0
                par = b % 2
                nc.vector.tensor_copy(score[:, par, :, KEYS], sink[:, :])
                for h, bank in ((0, ps_a), (1, ps_b)):
                    last = nc.vector.tensor_tensor_reduce(score[:, par, h, lo:KEYS], bank[:, lo:KEYS],
                                                          bias[:, h, lo:KEYS], 1.0, sink[:, h:h + 1], ALU.add,
                                                          ALU.max, top[:, par, h:h + 1])
                last.then_inc(att_biased, 1)
                dve.wait_ge(att_biased, CHUNKS * p + b + 1)
                nc.vector.tensor_scalar(ntop[:, par, :], top[:, par, :], -1.0, None,
                                        ALU.mult).then_inc(max_ready, 1)

            def att_scale(p, b):
                par = b % 4
                dve.wait_ge(exp_done, CHUNKS * p + b + 1)
                nc.vector.reciprocal(rsum[:, par, :], esum[:, par, :]).then_inc(rsum_ready, 1)
                dve.wait_ge(att_summed, CHUNKS * p + b + 1)
                dve.wait_ge(rsum_ready, CHUNKS * p + b + 1)
                nc.vector.scalar_tensor_tensor(
                    out=o_att[:, :].rearrange("p (h d) -> p h d", h=2),
                    in0=ps_e[:, 0:P].rearrange("p (h d) -> p h d", h=2), scalar=0.5,
                    in1=rsum[:, par, :].unsqueeze(2).to_broadcast([P, 2, 64]),
                    op0=ALU.mult, op1=ALU.mult).then_inc(oatt_scaled, 1)

            def att_start(p, j):
                nc.vector.tensor_copy(cb[:, :], cst[:, bass.ds(C_HEAD + N_HEAD * j, N_HEAD)]).then_inc(att_consts, 1)
                nc.vector.tensor_copy(sink[:, :], sink_all[:, :, bass.ds(j, 1)]).then_inc(att_consts, 1)
                dve.wait_ge(att_consts, 2 * p + 2)
                for h in range(2):
                    nc.vector.tensor_scalar(bias[:, h, :], cst[:, C_DIST:C_DIST + KEYS],
                                            cb[:, H_SLOPE + h:H_SLOPE + h + 1], None,
                                            ALU.mult).then_inc(bias_made, 1)
                dve.wait_ge(bias_made, 2 * p + 2)

            def att_steps(p, t, s):
                if s == 8:
                    combine("ag", p, 0)
                if 0 <= s - 3 < CHUNKS:
                    att_scale(p, s - 3)
                if s < CHUNKS:
                    att_bias(p, t, s)

            def phase_a(t, j, x_pre, x_main):
                ph = Phase("A", t, j)
                p = ph.p
                nc.vector.tensor_copy(ca[:, :], cst[:, bass.ds(C_HEAD + N_HEAD * j, N_HEAD)]).then_inc(ret_consts, 1)
                load_state(t, j, p)
                dve.wait_ge(ret_consts, p + 1)
                for s in range(12):
                    if s == 4:
                        make_gate("rg", p, 0)
                    if s == 6:
                        make_gate("ag", p, 0)
                    if s == 10:
                        make_gate("rg", p, 1)
                    if s in x_main:
                        x_low(x_main[s])
                    if 0 <= s - 1 < CHUNKS:
                        ret_state(p, s - 1)
                    if s < CHUNKS:
                        ret_mask(p, s)
                    if 0 <= s - 1 < CHUNKS:
                        ret_stats(p, s - 1)
                    if s == 4:
                        ret_var(p, 0)
                    if s == 6:
                        ret_norm(p, 0)
                    if s == 8:
                        ret_var(p, 1)
                        dve.wait_ge(state_ready, (CHUNKS + 1) * (p + 1))
                        combine("rg", p, 0)
                        nc.vector.tensor_copy(state_all[:, bass.ds(j, 1), :], state[:, :]).then_inc(state_saved, 1)
                    if s == 10:
                        ret_norm(p, 1)
                    for i in x_pre.get(s, ()):
                        x_norm(i)
                make_gate("ag", p, 1)
                combine("rg", p, 1)

            def phase_b(t, j, att_t, att_p, att_j):
                if att_p is None:
                    for s in range(4):
                        x_low(4 + s)
                        if 6 + s < 8:
                            x_norm(6 + s)
                    return
                att_start(att_p, att_j)
                for s in range(12):
                    att_steps(att_p, att_t, s)
                combine("ag", att_p, 1)

            dve.wait_ge(gain_in, 16)
            dve.wait_ge(const_in, 32)
            x_norm(0)
            x_norm(1)
            for i in range(4):
                x_low(i)
                x_norm(i + 2)
            for t in range(2):
                phase_b(t, 0, 0, None if t == 0 else 3, 3)
                with dve.Fori(0, HEADS - 1) as j:
                    phase_a(t, j, {}, {})
                    phase_b(t, j + 1, t, 4 * t + j, j)
                if t == 0:
                    phase_a(0, 3, {0: (8, 9), 1: (10,), 2: (11,), 3: (12,), 4: (13,), 6: (14,), 7: (15,)},
                            {1: 8, 2: 9, 3: 10, 4: 11, 6: 12, 7: 13, 8: 14, 9: 15})
                else:
                    phase_a(1, 3, {}, {})

            def out_finish(i):
                b, o = i % 2, out_sb[i % 2]
                dve.wait_ge(out_copied, 2 * i + 2)
                nc.vector.tensor_tensor(xss[:, b, 0:1], xss[:, b, 0:1], xss[:, b, 1:2],
                                        ALU.add).then_inc(out_ms, 1)
                dve.wait_ge(out_ms, i + 1)
                nc.vector.tensor_scalar(xz[:, b:b + 1], xss[:, b, 0:1], 1.0 / DM, EPS, ALU.mult,
                                        ALU.add).then_inc(out_var, 1)
                dve.wait_ge(out_rs, i + 1)
                nc.vector.scalar_tensor_tensor(out=o, in0=o, scalar=xr[:, b:b + 1], in1=gain[:, :],
                                               op0=ALU.mult, op1=ALU.mult).then_inc(out_scaled, 1)
                dve.wait_ge(out_scaled, i + 1)
                dve.wait_ge(res_in[b], 16 * (i // 2 + 1))
                nc.vector.tensor_tensor(o, o, xt[:, b, :], ALU.add).then_inc(out_added, 1)

            dve.wait_ge(gain_in, 32)
            att_start(7, 3)
            for s in range(12):
                if s in (6, 10):
                    out_finish(s // 4 - 1)
                att_steps(7, 1, s)
            combine("ag", 7, 1)
            for i in range(2, TILES):
                out_finish(i)


def shape_constants():
    import numpy as np

    c = np.zeros((P, C_ALL), np.float64)
    i = np.arange(P)
    c[:, C_MASK:C_MASK + P] = i[:, None] <= i[None, :]
    dist = i[:, None] + P - np.arange(KEYS)[None, :]
    c[:, C_DIST:C_DIST + KEYS] = np.where((dist >= 0) & (dist < P), -dist, -1e33)
    for j in range(HEADS):
        h = c[:, C_HEAD + N_HEAD * j:C_HEAD + N_HEAD * (j + 1)]
        decay = 1.0 - 2.0 ** (-5.0 - j)
        h[:, H_SLOPE] = 2.0 ** -(j + 1.0)
        h[:, H_SLOPE + 1] = 2.0 ** -(j + 5.0)
        h[:, H_GCINV] = decay ** -float(P)
        h[:, H_GC] = decay ** float(P)
        h[:, H_XI2] = decay ** (2.0 * (i + 1))
        h[:, H_XIH] = 0.5 * decay ** (i + 1.0)
        h[:, H_ZETA] = decay ** (P - 1.0 - i) * P ** -0.5
    return c.astype(np.float32)


def kernel(x, g_pre, w_in, sinks, w_out, g_post):
    import numpy as np
    import concourse.bacc as bacc
    from concourse.bass_utils import run_bass_kernel_spmd

    nc = bacc.Bacc("TRN2", target_bir_lowering=False, num_devices=1)
    arrays = {"x": np.ascontiguousarray(x).reshape(SEQ, DM), "g_pre": np.ascontiguousarray(g_pre),
              "w_in": np.ascontiguousarray(w_in), "sinks": np.ascontiguousarray(sinks),
              "w_out": np.ascontiguousarray(w_out), "g_post": np.ascontiguousarray(g_post),
              "consts": shape_constants()}
    args = [nc.dram_tensor(n, a.shape, F32, kind="ExternalInput").ap() for n, a in arrays.items()]
    mix = nc.dram_tensor("mix", (TILES, P, 2 * HEADS, P), F32, kind="Internal").ap()
    out = nc.dram_tensor("out", (SEQ, DM), F32, kind="ExternalOutput").ap()
    hybrid_layer(nc, *args, mix, out)
    r = run_bass_kernel_spmd(nc, [arrays], core_ids=[0])
    return r.results[0]["out"].reshape(1, SEQ, DM)
```

```python
from contextlib import ExitStack

import concourse.bass as bass
from concourse import mybir

F32 = mybir.dt.float32
F32R = mybir.dt.float32r
BF16 = mybir.dt.bfloat16
ALU = mybir.AluOpType
ACT = mybir.ActivationFunctionType

P = 128
SEQ = 2048
DM = 1024
KT = DM // P
SEC = 512
HALF = 1024
HEADS = 4
CHUNKS = HALF // P
PER_SEC = SEC // P
TILES = SEQ // P
EPS = 1e-6
NEG = -1e30
KEYS = 2 * P

COL = {"rq": 0, "rk": 512, "rv": 1024, "rg": 1536, "aq": 2048, "ak": 2560, "av": 2688, "ag": 2816}
A_UNITS = [("aq", 0), ("rg", 0), ("ag", 0), ("aq", 1), ("rg", 1), ("ag", 1)]
B_UNITS = [("rk", 0), ("rv", 0), ("rq", 0), ("rk", 1), ("rv", 1), ("rq", 1)]
K_UNITS = [("ak", 0), ("av", 0), ("ak", 1), ("av", 1)]
GROUPS = {"A": ["aq", "rg", "ag"], "B": ["rk", "rv", "rq"], "K": ["ak", "av"]}
HALF_GROUPS = 3 + 2 + 6 * HEADS - 3
HALF_UNITS = 2 * HALF_GROUPS
IN_GROUPS = 2 * HALF_GROUPS
OUT_CHUNKS = DM // P

C_MASK, C_DIST, C_HEAD, N_HEAD = 0, P, P + KEYS, 8
C_ALL = C_HEAD + HEADS * N_HEAD
H_SLOPE, H_GCINV, H_GC, H_XI2, H_XIH, H_ZETA = 0, 2, 3, 4, 5, 6


def wait_apart(eng, sem, count):
    if not isinstance(count, int):
        eng.wait_ge(sem, 1)
    eng.wait_ge(sem, count)


class Phase:

    def __init__(self, kind, t, j):
        self.kind, self.t, self.j = kind, t, j
        self.p = 4 * t + j
        self.groups = GROUPS[kind]
        self.n = len(self.groups)
        first = isinstance(j, int) and j == 0 and kind == "B"
        base = {"A": 5, "B": 0 if first else 2, "K": 3}[kind] + HALF_GROUPS * t
        steps = 0 if kind == "K" or first else j
        self.w0, self.w = base, base + 6 * steps
        self.u = 2 * base + 12 * steps

    def slot(self, g):
        return (self.w0 + g) % 3

    def raw(self, g):
        return (self.w0 + g) % 2

    def group_used(self, g):
        return self.u + self.n + g + 1


def nth(p, sec):
    return 2 * p + sec + 1


def hybrid_layer(nc, x, g_pre, w_in, sinks, w_out, g_post, consts, mix, out):
    ctx = ExitStack()
    with ctx:
        def sb(name, shape, dt=F32):
            return ctx.enter_context(nc.sbuf_tensor(name, shape, dt))

        def sem(name):
            return ctx.enter_context(nc.semaphore(name))

        cst = sb("cst", [P, C_ALL])
        ident = sb("ident", [P, P])
        gain = sb("gain", [P, DM])
        sink_all = sb("sink_all", [P, 2, HEADS])
        big = sb("big", [P, 3, 2, KT, SEC], F32R)
        wslot = sb("wslot", [P, 3, 2, KT, P], F32R)
        wraw = sb("wraw", [P, 2, KT, P])
        xt = sb("xt", [P, 4, DM])
        junk = sb("junk", [P, DM], BF16)
        rk_t = sb("rk_t", [P, HALF])
        rv_t = sb("rv_t", [P, HALF])
        rq_t = sb("rq_t", [P, HALF])
        aq_t = sb("aq_t", [P, HALF])
        gate = {"rg": sb("rgate", [P, HALF]), "ag": sb("agate", [P, HALF])}
        k_nat = sb("k_nat", [P, 2, P])
        v_nat = sb("v_nat", [P, 2, P])
        p_ret = sb("p_ret", [P, 2, P])
        state = sb("state", [P, P])
        state_all = sb("state_all", [P, HEADS, P])
        o_ret = sb("o_ret", [P, CHUNKS, P])
        ak_t = sb("ak_t", [P, (CHUNKS + 1) * P])
        av_n = sb("av_n", [P, CHUNKS + 1, P])
        bias = sb("bias", [P, 2, KEYS])
        score = sb("score", [P, 2, 2, KEYS + 1])
        p_t = sb("p_t", [P, 2, 2, P])
        o_att = sb("o_att", [P, P])
        ca = sb("ca", [P, N_HEAD])
        cb = sb("cb", [P, N_HEAD])
        cz = sb("cz", [P, 1])
        sink = sb("sink", [P, 2])
        bn = sb("bn", [P, CHUNKS, 6])
        mv = sb("mv", [P, CHUNKS, 2])
        zvar = sb("zvar", [P, CHUNKS])
        rvar = sb("rvar", [P, CHUNKS])
        rscale = sb("rscale", [P, CHUNKS])
        minus_half = sb("minus_half", [P, PER_SEC])
        top = sb("top", [P, 2, 2])
        ntop = sb("ntop", [P, 2, 2])
        esum = sb("esum", [P, 4, 2])
        rsum = sb("rsum", [P, 4, 2])
        xss = sb("xss", [P, 2, 2])
        xz = sb("xz", [P, 2])
        xr = sb("xr", [P, 2])
        credit = sb("credit", [P, 4])
        ticket = sb("ticket", [P, 1])

        proj = [ctx.enter_context(nc.psum_tensor(f"proj{i}", [P, SEC], F32)) for i in range(2)]
        ps_a, ps_b, ps_c, ps_d, ps_e, ps_f = [
            ctx.enter_context(nc.psum_tensor(f"ps_{i}", [P, SEC], F32)) for i in "abcdef"]

        const_in = sem("const_in")
        gain_in = sem("gain_in")
        ident_made = sem("ident_made")
        halves_made = sem("halves_made")
        x_in = [sem(f"x_in{i}") for i in range(4)]
        x_squared = sem("x_squared")
        x_var = sem("x_var")
        x_rs = sem("x_rs")
        x_normed = sem("x_normed")
        x_turned = sem("x_turned")
        x_hi = sem("x_hi")
        x_lo = sem("x_lo")
        raw_in = [sem(f"raw_in{i}") for i in range(2)]
        wout_in = [sem(f"wout_in{i}") for i in range(2)]
        w_hi = sem("w_hi")
        w_ready = sem("w_ready")
        w_out_ready = sem("w_out_ready")
        unit_done = sem("unit_done")
        copied = {k: sem(f"copied_{k}") for k in ("rk", "rv", "rq", "aq", "ak", "av")}
        tanh_done = {k: sem(f"tanh_{k}") for k in ("rg", "ag")}
        gated = {k: sem(f"gated_{k}") for k in ("rg", "ag")}
        v_turned = sem("v_turned")
        v_kept = sem("v_kept")
        ret_consts = sem("ret_consts")
        zeta_here = sem("zeta_here")
        ret_scored = sem("ret_scored")
        kv_copied = sem("kv_copied")
        ret_masked = sem("ret_masked")
        ret_summed = sem("ret_summed")
        o_copied = sem("o_copied")
        state_ready = sem("state_ready")
        state_saved = sem("state_saved")
        bn_done = sem("bn_done")
        aggr_done = sem("aggr_done")
        var_ready = sem("var_ready")
        rvar_ready = sem("rvar_ready")
        scale_ready = sem("scale_ready")
        o_normed = sem("o_normed")
        ret_turned = sem("ret_turned")
        combined = {k: sem(f"combined_{k}") for k in ("rg", "ag")}
        stored = {k: [sem(f"stored_{k}{i}") for i in range(2)] for k in ("rg", "ag")}
        att_consts = sem("att_consts")
        bias_made = sem("bias_made")
        att_scored = sem("att_scored")
        att_biased = sem("att_biased")
        max_ready = sem("max_ready")
        exp_done = sem("exp_done")
        p_turned = sem("p_turned")
        p_copied = sem("p_copied")
        rsum_ready = sem("rsum_ready")
        att_summed = sem("att_summed")
        oatt_scaled = sem("oatt_scaled")
        att_turned = sem("att_turned")
        mix_in = [sem(f"mix_in{i}") for i in range(2)]
        mix_hi = sem("mix_hi")
        mix_ready = sem("mix_ready")
        res_in = [sem(f"res_in{i}") for i in range(4)]
        out_done = sem("out_done")
        out_squared = sem("out_squared")
        out_copied = sem("out_copied")
        out_ms = sem("out_ms")
        out_var = sem("out_var")
        out_rs = sem("out_rs")
        out_added = sem("out_added")
        out_stored = [sem(f"out_stored{i}") for i in range(2)]

        w_in_v = w_in.rearrange("(k p) c -> p k c", p=P)
        w_out_v = w_out.rearrange("(k p) c -> p k c", p=P)
        w_out_pair = w_out[4 * P:, :].rearrange("(h k q) c -> h q k c", h=2, k=HEADS)
        n_tok = {"rg": 0, "ag": HEADS}

        def hbuf(t, sec):
            return (2 * t + sec) % 3

        mix_raw = [rk_t[:, :], rv_t[:, :]]
        out_sb = [rq_t[:, :], o_ret[:, :, :].rearrange("p c d -> p (c d)")]

        def mix_split(i, part):
            return big[:, 2, part, :, P * (i % 4):P * (i % 4) + P]

        def w_out_at(c):
            return 1 if c == 0 else 0

        def w_out_parts(q):
            cols = slice(P * (q % 4), P * (q % 4) + P)
            return [big[:, w_out_at(q // 4), part, :, cols] for part in range(2)]

        def x_banks(i):
            return (ps_c, ps_d) if i < 12 and i % 2 == 0 else (ps_e, ps_f)

        out_units = [(0, 0), (1, 0), (0, 1), (1, 1)] + [(i, c) for i in range(2, TILES) for c in range(2)]
        out_banks = [proj[0], proj[1], ps_f]

        def tile_done(i):
            return out_units.index((i, 1)) + 1

        block = ctx.enter_context(nc.Block())

        @block.sync
        def _(sp):
            def load_w(ph, g):
                kind, j, b = ph.groups[g], ph.j, ph.raw(g)
                if not (isinstance(ph.w, int) and ph.w + g < 2):
                    sp.wait_ge(w_ready, ph.w + g - 1)
                dst = wraw[:, b, :, :]
                if kind in ("aq", "ag"):
                    for h in range(2):
                        src = w_in_v[:, :, bass.ds(COL[kind] + 256 * h + 64 * j, 64)]
                        sp.dma_start(dst[:, :, 64 * h:64 * h + 64], src).then_inc(raw_in[b], 16)
                else:
                    col = COL[kind] if kind in ("ak", "av") else COL[kind] + P * j
                    for h in (1, 0):
                        src = w_in_v[:, 4 * h:4 * h + 4, bass.ds(col, P)]
                        sp.dma_start(dst[:, 4 * h:4 * h + 4, :], src).then_inc(raw_in[b], 16)

            def load_x(i):
                if i >= 4:
                    sp.wait_ge(x_turned, i - 3)
                sp.dma_start(xt[:, i % 4, :], x[i * P:(i + 1) * P, :]).then_inc(x_in[i % 4], 16)

            def store(kind, t, j, sec):
                sp.wait_ge(combined[kind], nth(4 * t + j, sec))
                tile = PER_SEC * (2 * t + sec)
                dst = mix[tile:tile + PER_SEC, :, bass.ds(n_tok[kind] + j, 1), :]
                sp.dma_start(dst.rearrange("i p g n -> p (i g) n"),
                             gate[kind][:, SEC * sec:SEC * (sec + 1)].rearrange("p (i n) -> p i n", n=P)
                             ).then_inc(stored[kind][sec], 16)

            def load_w_out(q):
                b = (IN_GROUPS + q) % 2
                if q < 6:
                    sp.wait_ge(w_ready, IN_GROUPS + q - 1)
                else:
                    sp.wait_ge(w_out_ready, q - 5)
                cols = slice(q * P, (q + 1) * P)
                sp.dma_start(wraw[:, b, 0:4, :], w_out_v[:, 0:4, cols]).then_inc(wout_in[b], 16)
                for h in range(2):
                    sp.dma_start(wraw[64 * h:64 * h + 64, b, 4:8, :],
                                 w_out_pair[h, :, :, cols]).then_inc(wout_in[b], 16)

            first = Phase("B", 0, 0)
            load_x(0)
            sp.dma_start(gain[:, :], g_pre.partition_broadcast(P)).then_inc(gain_in, 16)
            load_x(1)
            load_x(2)
            load_w(first, 0)
            load_x(3)
            load_w(first, 1)
            load_x(4)
            load_x(5)
            load_x(6)
            sp.dma_start(cst[:, :], consts).then_inc(const_in, 16)
            sp.dma_start(sink_all[:, :, :].rearrange("p a b -> p (a b)"),
                         sinks.partition_broadcast(P)).then_inc(const_in, 16)
            load_w(first, 2)
            load_x(7)
            for t in range(2):
                nxt = Phase("K", t, 0)
                if t == 0:
                    for i in range(8, 12):
                        load_x(i)
                load_w(nxt, 0)
                load_w(nxt, 1)
                if t == 1:
                    store("ag", 0, 3, 0)
                    store("ag", 0, 3, 1)
                nxt = Phase("A", t, 0)
                for g in range(3):
                    load_w(nxt, g)
                    if t == 0 and g < 2:
                        load_x(12 + 2 * g)
                        load_x(13 + 2 * g)
                with sp.Fori(0, HEADS - 1) as j:
                    nxt = Phase("B", t, j + 1)
                    load_w(nxt, 0)
                    load_w(nxt, 1)
                    store("rg", t, j, 0)
                    load_w(nxt, 2)
                    store("rg", t, j, 1)
                    nxt = Phase("A", t, j + 1)
                    load_w(nxt, 0)
                    load_w(nxt, 1)
                    store("ag", t, j, 0)
                    load_w(nxt, 2)
                    store("ag", t, j, 1)
                if t == 0:
                    nxt = Phase("B", 1, 0)
                    load_w(nxt, 0)
                    load_w(nxt, 1)
                    store("rg", 0, 3, 0)
                    load_w(nxt, 2)
                    store("rg", 0, 3, 1)

            def load_mix(i):
                if i >= 2:
                    sp.wait_ge(mix_ready, i - 1)
                else:
                    sp.wait_ge(ret_summed, 8 * CHUNKS)
                sp.dma_start(mix_raw[i % 2].rearrange("p (g n) -> p g n", n=P),
                             mix[i, :, :, :]).then_inc(mix_in[i % 2], 16)

            def load_res(i):
                if i >= 4:
                    sp.wait_ge(out_added, i - 3)
                else:
                    sp.wait_ge(x_turned, TILES)
                sp.dma_start(xt[:, i % 4, :], x[i * P:(i + 1) * P, :]).then_inc(res_in[i % 4], 16)

            def store_out(i):
                if i < TILES - 1:
                    sp.wait_ge(out_added, i + 1)
                    sp.dma_start(out[i * P:(i + 1) * P, :], out_sb[i % 2]).then_inc(out_stored[i % 2], 16)
                    return
                for c in range(2):
                    cols = slice(SEC * c, SEC * (c + 1))
                    sp.wait_ge(out_added, i + c + 1)
                    sp.dma_start(out[i * P:(i + 1) * P, cols], out_sb[i % 2][:, cols]
                                 ).then_inc(out_stored[i % 2], 16)

            sp.wait_ge(x_normed, TILES)
            sp.dma_start(gain[:, :], g_post.partition_broadcast(P)).then_inc(gain_in, 16)
            for q in range(6):
                load_w_out(q)
            for i in range(3):
                load_res(i)
            store("rg", 1, 3, 0)
            for sec in range(2):
                for k in ("rg", "ag"):
                    sp.wait_ge(stored[k][sec], 16 * (HEADS + 1))
            load_mix(0)
            load_mix(1)
            store("rg", 1, 3, 1)
            load_w_out(6)
            load_w_out(7)
            load_mix(2)
            load_mix(3)
            for i in range(TILES):
                if i + 4 < TILES:
                    if i + 4 == TILES // 2:
                        for sec in range(2):
                            for k in ("rg", "ag"):
                                sp.wait_ge(stored[k][sec], 16 * (2 * HEADS + 1))
                    load_mix(i + 4)
                store_out(i)
                if i + 3 < TILES:
                    load_res(i + 3)
                if i in (1, 2):
                    store("ag", 1, 3, i - 1)
            sp.wait_ge(out_stored[0], 16 * TILES // 2)
            sp.wait_ge(out_stored[1], 16 * (TILES // 2 + 1))

        @block.gpsimd
        def _(pool):
            nc.gpsimd.memset(minus_half[:, :], -0.5).then_inc(halves_made, 1)
            nc.gpsimd.memset(ident[:, :], 0.0).then_inc(ident_made, 1)
            pool.wait_ge(ident_made, 1)
            nc.gpsimd.affine_select(out=ident[:, :], in_=ident[:, :], compare_op=ALU.not_equal, fill=1.0,
                                    base=0, pattern=[[-1, P]], channel_multiplier=1).then_inc(ident_made, 1)

            def split_group(ph, g, used):
                s, b = ph.slot(g), ph.raw(g)
                pool.wait_ge(raw_in[b], 32 * ((ph.w0 + g) // 2 + 1) + 16 * (ph.w - ph.w0))
                if used is not None:
                    pool.wait_ge(unit_done, used)
                nc.gpsimd.tensor_tensor(ticket[:, :], minus_half[:, 0:1], minus_half[:, 0:1], ALU.mult)
                nc.gpsimd.tensor_copy(wslot[:, s, 0, :, :], wraw[:, b, :, :]).then_inc(w_hi, 1)
                pool.wait_ge(w_hi, ph.w + g + 1)
                nc.gpsimd.tensor_tensor(wslot[:, s, 1, :, :], wraw[:, b, :, :], wslot[:, s, 0, :, :],
                                        ALU.subtract).then_inc(w_ready, 1)

            def split_low(sem_in, count, dst, w):
                pool.wait_ge(sem_in, count)
                pool.wait_ge(w_hi, w + 1)
                nc.gpsimd.tensor_tensor(dst[1], wraw[:, w % 2, :, :], dst[0], ALU.subtract).then_inc(w_ready, 1)

            def x_power(i):
                pool.wait_ge(x_var, i + 1)
                nc.gpsimd.tensor_tensor(xr[:, i % 2:i % 2 + 1], xz[:, i % 2:i % 2 + 1],
                                        minus_half[:, 0:1], ALU.pow).then_inc(x_rs, 1)

            def ret_power(p, sec):
                pool.wait_ge(var_ready, nth(p, sec))
                cs = slice(PER_SEC * sec, PER_SEC * (sec + 1))
                nc.gpsimd.tensor_tensor(rvar[:, cs], zvar[:, cs], minus_half[:, :],
                                        ALU.pow).then_inc(rvar_ready, 1)

            pool.wait_ge(halves_made, 1)
            first = Phase("B", 0, 0)
            for i in range(4):
                x_power(i)
            for g in range(3):
                split_low(raw_in[g % 2], 32 * (g // 2 + 1),
                          (wslot[:, g, 0, :, :], wslot[:, g, 1, :, :]), g)
                for i in ((4,), (5, 6), (7,))[g]:
                    x_power(i)
            for i in range(8, 12):
                x_power(i)
            for t in range(2):
                cur, nxt = Phase("B", t, 0), Phase("K", t, 0)
                for g in range(2):
                    split_group(nxt, g, cur.group_used(g))
                cur, nxt = nxt, Phase("A", t, 0)
                split_group(nxt, 0, cur.u)
                if t == 0:
                    for i in range(12, 16):
                        x_power(i)
                split_group(nxt, 1, cur.group_used(0))
                split_group(nxt, 2, cur.group_used(1))
                with pool.Fori(0, HEADS - 1) as j:
                    cur, nxt = Phase("A", t, j), Phase("B", t, j + 1)
                    ret_power(cur.p, 0)
                    split_group(nxt, 0, cur.group_used(0))
                    ret_power(cur.p, 1)
                    split_group(nxt, 1, cur.group_used(1))
                    split_group(nxt, 2, cur.group_used(2))
                    cur, nxt = nxt, Phase("A", t, j + 1)
                    for g in range(3):
                        split_group(nxt, g, cur.group_used(g))
                if t == 0:
                    cur, nxt = Phase("A", 0, 3), Phase("B", 1, 0)
                    ret_power(3, 0)
                    split_group(nxt, 0, cur.group_used(0))
                    ret_power(3, 1)
                    split_group(nxt, 1, cur.group_used(1))
                    split_group(nxt, 2, cur.group_used(2))

            def split_mix_low(i):
                pool.wait_ge(mix_hi, i + 1)
                nc.gpsimd.tensor_tensor(mix_split(i, 1), mix_raw[i % 2].rearrange("p (g n) -> p g n", n=P),
                                        mix_split(i, 0), ALU.subtract).then_inc(mix_ready, 1)

            def out_power(i):
                pool.wait_ge(out_var, i + 1)
                nc.gpsimd.tensor_tensor(xr[:, i % 2:i % 2 + 1], xz[:, i % 2:i % 2 + 1],
                                        minus_half[:, 0:1], ALU.pow).then_inc(out_rs, 1)

            for q in range(4):
                split_low(wout_in[(IN_GROUPS + q) % 2], 48 * (q // 2 + 1), w_out_parts(q), IN_GROUPS + q)
                if q in (1, 3):
                    ret_power(7, q // 2)
            for i in range(3):
                split_mix_low(i)
            for i in range(TILES):
                out_power(i)
                if i + 3 < TILES:
                    split_mix_low(i + 3)

        @block.tensor
        def _(pe):
            def turn_x(i):
                pe.wait_ge(x_normed, i + 1)
                if i >= 12:
                    pe.wait_ge(x_lo, 2 * i)
                elif i >= 2:
                    pe.wait_ge(x_lo, 2 * (i - 1))
                for k in range(KT):
                    last = nc.tensor.transpose(x_banks(i)[k // 4][:, P * (k % 4):P * (k % 4) + P],
                                               xt[:, i % 4, P * k:P * (k + 1)], ident[:, :])
                last.then_inc(x_turned, 1)

            def unit_half(ph, units, s, bank_free):
                u, half = divmod(s, 2)
                kind, sec = units[u]
                g = ph.groups.index(kind)
                if half == 0:
                    if bank_free is not None:
                        pe.wait_ge(*bank_free)
                    if sec == 0:
                        pe.wait_ge(w_ready, ph.w + g + 1)
                w, h = ph.slot(g), hbuf(ph.t, sec)
                bank = proj[u % 2]
                for k in range(4 * half, 4 * half + 4):
                    for wp, hp in ((0, 0), (0, 1), (1, 0)):
                        last = nc.tensor.matmul(bank[:, :], wslot[:, w, wp, k, :], big[:, h, hp, k, :],
                                                start=(k == 0 and wp + hp == 0), stop=(k == KT - 1 and wp == 1))
                if half == 1:
                    last.then_inc(unit_done, 1)

            def evacuated(kind, sec, p):
                return (gated if kind in gated else copied)[kind], nth(p, sec)

            def ret_score(p, c):
                sec, par = c // PER_SEC, slice(c * P, (c + 1) * P)
                if c % PER_SEC == 0:
                    for k in ("rk", "rv", "rq"):
                        pe.wait_ge(copied[k], nth(p, sec))
                nc.tensor.transpose(ps_a[:, 0:P], rk_t[:, par], ident[:, :])
                nc.tensor.transpose(ps_a[:, P:2 * P], rv_t[:, par], ident[:, :])
                nc.tensor.matmul(ps_b[:, 0:P], rk_t[:, par], rq_t[:, par],
                                 start=True, stop=True).then_inc(ret_scored, 1)

            def ret_sum(p, c):
                n = CHUNKS * p + c
                pe.wait_ge(kv_copied, n + 1)
                pe.wait_ge(ret_masked, n + 1)
                pe.wait_ge(state_ready, (CHUNKS + 1) * p + c + 1)
                nc.tensor.matmul(ps_c[:, P:2 * P], k_nat[:, c % 2, :], v_nat[:, c % 2, :], start=True, stop=True)
                nc.tensor.matmul(ps_c[:, 0:P], p_ret[:, c % 2, :], v_nat[:, c % 2, :], start=True, stop=False)
                nc.tensor.matmul(ps_c[:, 0:P], rq_t[:, c * P:(c + 1) * P], state[:, :],
                                 start=False, stop=True).then_inc(ret_summed, 1)

            def ret_turn(p, sec):
                pe.wait_ge(o_normed, nth(p, sec))
                for c in range(PER_SEC):
                    last = nc.tensor.transpose(ps_d[:, c * P:(c + 1) * P], o_ret[:, PER_SEC * sec + c, :],
                                               ident[:, :])
                last.then_inc(ret_turned, 1)

            def att_score(p, t, b):
                if b % PER_SEC == 0:
                    pe.wait_ge(copied["aq"], nth(p, b // PER_SEC))
                    pe.wait_ge(copied["ak"], nth(t, 1))
                if b >= 1:
                    pe.wait_ge(att_biased, CHUNKS * p + b)
                lo = P if t == 0 and b == 0 else 0
                for h, bank in ((0, ps_a), (1, ps_b)):
                    rows = slice(64 * h, 64 * h + 64)
                    last = nc.tensor.matmul(bank[:, lo:KEYS], aq_t[rows, b * P:(b + 1) * P],
                                            ak_t[rows, b * P + lo:b * P + KEYS], start=True, stop=True)
                last.then_inc(att_scored, 1)

            def att_turn_p(p, t, b):
                pe.wait_ge(exp_done, CHUNKS * p + b + 1)
                for h in range(2):
                    for e in range(1 if t == 0 and b == 0 else 0, 2):
                        at = P * (2 * h + e)
                        last = nc.tensor.transpose(ps_c[:, at:at + P], score[:, b % 2, h, P * e:P * (e + 1)],
                                                   ident[:, :])
                last.then_inc(p_turned, 1)

            def att_sum(p, t, b):
                pe.wait_ge(p_copied, CHUNKS * p + b + 1)
                if b == 0:
                    pe.wait_ge(v_kept, nth(t, 1))
                es = (1,) if t == 0 and b == 0 else (0, 1)
                for h in range(2):
                    for e in es:
                        last = nc.tensor.matmul(ps_e[:, 64 * h:64 * h + 64], p_t[:, h, e, :],
                                                av_n[:, b + e, 64 * h:64 * h + 64],
                                                start=(e == es[0]), stop=(e == 1))
                last.then_inc(att_summed, 1)

            def att_turn_o(p, b):
                pe.wait_ge(oatt_scaled, CHUNKS * p + b + 1)
                if b % PER_SEC == 0:
                    if b == 0:
                        pe.wait_ge(combined["rg"], nth(p, 1))
                    else:
                        pe.wait_ge(combined["ag"], nth(p, 0))
                nc.tensor.transpose(ps_d[:, P * (b % PER_SEC):P * (b % PER_SEC) + P], o_att[:, :],
                                    ident[:, :]).then_inc(att_turned, 1)

            def att_steps(p, t, s):
                if 0 <= s - 4 < CHUNKS:
                    att_turn_o(p, s - 4)
                if 0 <= s - 3 < CHUNKS:
                    att_sum(p, t, s - 3)
                if 0 <= s - 2 < CHUNKS:
                    att_turn_p(p, t, s - 2)
                if s < CHUNKS:
                    att_score(p, t, s)

            def phase_a(t, j, x_tiles):
                ph = Phase("A", t, j)
                for s in range(12):
                    if s == 7:
                        ret_turn(ph.p, 0)
                    if 0 <= s - 1 < CHUNKS:
                        ret_sum(ph.p, s - 1)
                    if s < CHUNKS:
                        ret_score(ph.p, s)
                    if s == 11:
                        pe.wait_ge(combined["rg"], nth(ph.p, 0))
                        ret_turn(ph.p, 1)
                    if s in x_tiles:
                        turn_x(x_tiles[s])
                    u = s // 2
                    if u >= 2:
                        free = evacuated(*A_UNITS[u - 2], ph.p)
                    else:
                        free = evacuated(*B_UNITS[4 + u], ph.p)
                    unit_half(ph, A_UNITS, s, free)

            def phase_b(t, j, att_t, att_p):
                ph = Phase("B", t, j)
                for s in range(12):
                    if att_p is not None:
                        att_steps(att_p, att_t, s)
                    elif s < 4:
                        turn_x(4 + s)
                    u = s // 2
                    if s in (0, 6) and isinstance(j, int) and j == 0:
                        pe.wait_ge(x_lo, 2 * PER_SEC * (2 * t + s // 6 + 1))
                    if u >= 2:
                        free = evacuated(*B_UNITS[u - 2], ph.p)
                    elif att_p is not None:
                        free = evacuated(*A_UNITS[4 + u], att_p)
                    else:
                        free = None
                    unit_half(ph, B_UNITS, s, free)

            def turn_v(t, sec):
                pe.wait_ge(copied["av"], nth(t, sec))
                if sec == 1:
                    pe.wait_ge(v_kept, nth(t, 0))
                for b in range(PER_SEC):
                    at = SEC * sec + P * b
                    last = nc.tensor.transpose(ps_f[:, P * b:P * (b + 1)], aq_t[:, at:at + P], ident[:, :])
                last.then_inc(v_turned, 1)

            def phase_k(t):
                ph = Phase("K", t, 0)
                for s in range(8):
                    if t == 0 and s < 4:
                        turn_x(8 + s)
                    if s == 5:
                        if t == 0:
                            pe.wait_ge(x_lo, 24)
                        turn_v(t, 0)
                    u = s // 2
                    free = evacuated(*K_UNITS[u - 2], t) if u >= 2 else evacuated(*B_UNITS[4 + u], ph.p)
                    unit_half(ph, K_UNITS, s, free)
                pe.wait_ge(copied["ak"], nth(t, 1))
                turn_v(t, 1)

            pe.wait_ge(ident_made, 2)
            for i in range(4):
                turn_x(i)
            for t in range(2):
                phase_b(t, 0, 0, None if t == 0 else 3)
                phase_k(t)
                with pe.Fori(0, HEADS - 1) as j:
                    phase_a(t, j, {})
                    phase_b(t, j + 1, t, 4 * t + j)
                phase_a(t, 3, {6: 12, 7: 13, 8: 14, 9: 15} if t == 0 else {})

            def out_half(n, half):
                i, c = out_units[n]
                bank = out_banks[n % 3]
                if half == 0:
                    if c == 0:
                        pe.wait_ge(mix_ready, i + 1)
                    if n < 2:
                        pe.wait_ge(*evacuated(*A_UNITS[4 + n], 7))
                    elif n == 2:
                        pe.wait_ge(v_kept, nth(1, 1))
                    else:
                        pe.wait_ge(out_copied, n - 2)
                    if n == 0:
                        pe.wait_ge(w_ready, IN_GROUPS + 4)
                    if n == 2:
                        pe.wait_ge(w_out_ready, 4)
                for k in range(4 * half, 4 * half + 4):
                    for mp, wp in ((0, 0), (0, 1), (1, 0)):
                        last = nc.tensor.matmul(bank[:, :], mix_split(i, mp)[:, k, :],
                                                big[:, w_out_at(c), wp, k, :],
                                                start=(k == 0 and mp + wp == 0), stop=(k == KT - 1 and mp == 1))
                if half == 1:
                    last.then_inc(out_done, 1)

            for n in range(2 * TILES):
                for half in range(2):
                    if 2 * n + half < 12:
                        att_steps(7, 1, 2 * n + half)
                    out_half(n, half)

        @block.scalar
        def _(act):
            def x_square(i):
                act.wait_ge(x_in[i % 4], 16 * (i // 4 + 1))
                if i >= 2:
                    act.wait_ge(x_var, i - 1)
                if i >= 1:
                    act.wait_ge(x_squared, i)
                nc.scalar.activation(junk[:, :], xt[:, i % 4, :], ACT.Square,
                                     accum_out=xss[:, i % 2, 0:1]).then_inc(x_squared, 1)

            def x_high(i):
                b, at = (i // PER_SEC) % 3, P * (i % PER_SEC)
                act.wait_ge(x_turned, i + 1)
                if i == 12:
                    act.wait_ge(unit_done, Phase("A", 0, 3).u + 3)
                for h, bank in enumerate(x_banks(i)):
                    nc.scalar.copy(big[:, b, 0, 4 * h:4 * h + 4, at:at + P],
                                   bank[:, :].rearrange("p (k n) -> p k n", n=P)).then_inc(x_hi, 1)

            def split_high(w, sem_in, count, dst):
                act.wait_ge(sem_in, count)
                nc.scalar.copy(dst[0], wraw[:, w % 2, :, :]).then_inc(w_hi, 1)

            def first_high(g):
                split_high(g, raw_in[g % 2], 32 * (g // 2 + 1), [wslot[:, g, 0, :, :]])

            def w_out_high(q):
                w = IN_GROUPS + q
                if q == 4:
                    act.wait_ge(unit_done, 2 * HALF_UNITS)
                if q == 0:
                    act.wait_ge(w_ready, w)
                split_high(w, wout_in[w % 2], 48 * (q // 2 + 1), w_out_parts(q))

            def mix_high(i):
                act.wait_ge(mix_in[i % 2], 16 * (i // 2 + 1))
                if i >= 4:
                    act.wait_ge(out_done, tile_done(i - 4))
                elif i == 0:
                    act.wait_ge(unit_done, 2 * HALF_UNITS - 3)
                nc.scalar.copy(mix_split(i, 0), mix_raw[i % 2].rearrange("p (g n) -> p g n", n=P)
                               ).then_inc(mix_hi, 1)

            def evacuate(ph, units, u):
                kind, sec = units[u]
                bank, cols = proj[u % 2], slice(SEC * sec, SEC * (sec + 1))
                act.wait_ge(unit_done, ph.u + u + 1)
                if kind in ("rg", "ag"):
                    act.wait_ge(stored[kind][sec], 16 * ph.p + 16)
                    nc.scalar.activation(gate[kind][:, cols], bank[:, :], ACT.Tanh,
                                         scale=0.5).then_inc(tanh_done[kind], 1)
                    return
                dst = {"rk": rk_t, "rv": rv_t, "rq": rq_t, "aq": aq_t, "av": aq_t, "ak": ak_t}[kind]
                if kind == "ak":
                    cols = slice(P + SEC * sec, P + SEC * (sec + 1))
                if kind == "aq":
                    nc.scalar.activation(dst[:, cols], bank[:, :], ACT.Copy,
                                         scale=0.125).then_inc(copied[kind], 1)
                else:
                    nc.scalar.copy(dst[:, cols], bank[:, :]).then_inc(copied[kind], 1)

            def ret_copies(p, c):
                act.wait_ge(ret_scored, CHUNKS * p + c + 1)
                nc.scalar.copy(k_nat[:, c % 2, :], ps_a[:, 0:P])
                nc.scalar.activation(v_nat[:, c % 2, :], ps_a[:, P:2 * P], ACT.Copy,
                                     scale=cz[:, 0:1]).then_inc(kv_copied, 1)

            def att_exp(p, t, b):
                act.wait_ge(max_ready, CHUNKS * p + b + 1)
                lo = P if t == 0 and b == 0 else 0
                for h in range(2):
                    s = score[:, b % 2, h, lo:KEYS + 1]
                    last = nc.scalar.activation(s, s, ACT.Exp, bias=ntop[:, b % 2, h:h + 1],
                                                accum_out=esum[:, b % 4, h:h + 1])
                last.then_inc(exp_done, 1)

            def att_copy_p(p, t, b):
                act.wait_ge(p_turned, CHUNKS * p + b + 1)
                lo = 1 if t == 0 and b == 0 else 0
                nc.scalar.copy(p_t[:, :, lo:2, :],
                               ps_c[:, :].rearrange("p (h e n) -> p h e n", h=2, e=2)[:, :, lo:2, :]
                               ).then_inc(p_copied, 1)

            def att_steps(p, t, s):
                if 0 <= s - 2 < CHUNKS:
                    att_copy_p(p, t, s - 2)
                if s < CHUNKS:
                    att_exp(p, t, s)

            def phase_a(t, j, extra):
                ph = Phase("A", t, j)
                nc.scalar.copy(cz[:, 0:1], cst[:, bass.ds(C_HEAD + H_ZETA + N_HEAD * j, 1)]).then_inc(zeta_here, 1)
                for s in range(12):
                    if s >= 2 and s % 2 == 0:
                        evacuate(ph, A_UNITS, s // 2 - 1)
                    if s < CHUNKS:
                        if s == 0:
                            act.wait_ge(zeta_here, ph.p + 1)
                        ret_copies(ph.p, s)
                    for step, i in extra.get(s, ()):
                        step(i)
                evacuate(ph, A_UNITS, 5)

            def phase_b(t, j, att_t, att_p):
                ph = Phase("B", t, j)
                for s in range(12):
                    if s >= 2 and s % 2 == 0:
                        evacuate(ph, B_UNITS, s // 2 - 1)
                    if att_p is not None:
                        att_steps(att_p, att_t, s)
                    elif s < 4:
                        x_high(4 + s)
                        if s == 0:
                            x_square(7)
                        if s == 1:
                            first_high(2)
                    if att_p is None and 3 <= s < 7:
                        x_square(5 + s)
                evacuate(ph, B_UNITS, 5)

            def keep_v(t, sec):
                act.wait_ge(v_turned, nth(t, sec))
                nc.scalar.copy(av_n[:, 1 + PER_SEC * sec:1 + PER_SEC * (sec + 1), :],
                               ps_f[:, :].rearrange("p (b n) -> p b n", n=P)).then_inc(v_kept, 1)

            def phase_k(t):
                ph = Phase("K", t, 0)
                if t == 1:
                    act.wait_ge(att_summed, 4 * CHUNKS)
                    nc.scalar.copy(ak_t[:, 0:P], ak_t[:, CHUNKS * P:(CHUNKS + 1) * P])
                    nc.scalar.copy(av_n[:, 0, :], av_n[:, CHUNKS, :])
                for s in range(8):
                    if s >= 2 and s % 2 == 0:
                        evacuate(ph, K_UNITS, s // 2 - 1)
                    if s == 5:
                        keep_v(t, 0)
                    if t == 0:
                        if s < 4:
                            x_high(8 + s)
                        if 2 <= s < 6:
                            x_square(10 + s)
                evacuate(ph, K_UNITS, 3)
                keep_v(t, 1)

            for i in range(3):
                x_square(i)
            for i in range(4):
                x_high(i)
                x_square(i + 3)
                if i in (1, 3):
                    first_high(i // 2)
            act.wait_ge(const_in, 32)
            for t in range(2):
                phase_b(t, 0, 0, None if t == 0 else 3)
                phase_k(t)
                with act.Fori(0, HEADS - 1) as j:
                    phase_a(t, j, {})
                    phase_b(t, j + 1, t, 4 * t + j)
                if t == 0:
                    phase_a(0, 3, {6: [(x_high, 12)], 7: [(x_high, 13)], 8: [(x_high, 14)], 9: [(x_high, 15)]})
                else:
                    phase_a(1, 3, {1: [(w_out_high, 0)], 2: [(w_out_high, 1)], 4: [(w_out_high, 2)],
                                   5: [(w_out_high, 3)], 10: [(mix_high, 0)], 11: [(mix_high, 1)]})

            def out_square(n):
                i, c = out_units[n]
                act.wait_ge(out_done, n + 1)
                if i >= 2 and c == 0:
                    act.wait_ge(out_ms, i - 1)
                if n >= 1:
                    act.wait_ge(out_squared, n)
                else:
                    act.wait_ge(x_squared, TILES)
                nc.scalar.activation(junk[:, 0:SEC], out_banks[n % 3][:, :], ACT.Square,
                                     accum_out=xss[:, i % 2, c:c + 1]).then_inc(out_squared, 1)

            w_out_high(4)
            w_out_high(5)
            for n in range(2 * TILES):
                for half in range(2):
                    s = 2 * n + half
                    if s < 12:
                        att_steps(7, 1, s)
                    if half == 0 and n >= 1:
                        out_square(n - 1)
                    if s in (1, 2):
                        w_out_high(5 + s)
                    if s in (3, 7):
                        mix_high(2 + s // 7)
                    if half == 1 and n >= 4 and n % 2 == 0 and n // 2 + 2 < TILES:
                        mix_high(n // 2 + 2)
            out_square(2 * TILES - 1)

        @block.vector
        def _(dve):
            for i, (k, sec) in enumerate((k, sec) for k in ("rg", "ag") for sec in range(2)):
                nc.vector.memset(credit[:, i:i + 1], 0.0).then_inc(stored[k][sec], 16)

            def x_norm(i):
                b = i % 2
                dve.wait_ge(x_squared, i + 1)
                if i >= 2:
                    dve.wait_ge(x_rs, i - 1)
                nc.vector.tensor_scalar(xz[:, b:b + 1], xss[:, b, 0:1], 1.0 / DM, EPS, ALU.mult,
                                        ALU.add).then_inc(x_var, 1)
                dve.wait_ge(x_rs, i + 1)
                nc.vector.scalar_tensor_tensor(out=xt[:, i % 4, :], in0=xt[:, i % 4, :],
                                               scalar=xr[:, b:b + 1], in1=gain[:, :], op0=ALU.mult,
                                               op1=ALU.mult).then_inc(x_normed, 1)

            def x_low(i):
                b, at = (i // PER_SEC) % 3, P * (i % PER_SEC)
                for h, bank in enumerate(x_banks(i)):
                    ks = slice(4 * h, 4 * h + 4)
                    dve.wait_ge(x_hi, 2 * i + h + 1)
                    nc.vector.tensor_tensor(big[:, b, 1, ks, at:at + P],
                                            bank[:, :].rearrange("p (k n) -> p k n", n=P),
                                            big[:, b, 0, ks, at:at + P], ALU.subtract).then_inc(x_lo, 1)

            def make_gate(kind, p, sec):
                g = gate[kind][:, SEC * sec:SEC * (sec + 1)]
                bank = proj[A_UNITS.index((kind, sec)) % 2]
                dve.wait_ge(tanh_done[kind], nth(p, sec))
                nc.vector.scalar_tensor_tensor(out=g, in0=g, scalar=1.0, in1=bank[:, :], op0=ALU.add,
                                               op1=ALU.mult).then_inc(gated[kind], 1)

            def combine(kind, p, sec):
                g = gate[kind][:, SEC * sec:SEC * (sec + 1)]
                if kind == "rg":
                    dve.wait_ge(ret_turned, nth(p, sec))
                else:
                    dve.wait_ge(att_turned, CHUNKS * p + PER_SEC * (sec + 1))
                dve.wait_ge(gated[kind], nth(p, sec))
                nc.vector.tensor_tensor(g, ps_d[:, :], g, ALU.mult).then_inc(combined[kind], 1)

            def load_state(t, j, p):
                if t == 0:
                    nc.vector.memset(state[:, :], 0.0).then_inc(state_ready, 1)
                else:
                    dve.wait_ge(state_saved, HEADS)
                    nc.vector.tensor_copy(state[:, :], state_all[:, bass.ds(j, 1), :]).then_inc(state_ready, 1)

            def ret_mask(p, c):
                dve.wait_ge(ret_scored, CHUNKS * p + c + 1)
                nc.vector.scalar_tensor_tensor(out=p_ret[:, c % 2, :], in0=ps_b[:, 0:P],
                                               scalar=ca[:, H_GCINV:H_GCINV + 1], in1=cst[:, C_MASK:C_MASK + P],
                                               op0=ALU.mult, op1=ALU.mult).then_inc(ret_masked, 1)

            def ret_state(p, c):
                dve.wait_ge(ret_summed, CHUNKS * p + c + 1)
                nc.vector.tensor_copy(o_ret[:, c, :], ps_c[:, 0:P]).then_inc(o_copied, 1)
                dve.wait_ge(state_ready, (CHUNKS + 1) * p + c + 1)
                nc.vector.scalar_tensor_tensor(out=state[:, :], in0=state[:, :], scalar=ca[:, H_GC:H_GC + 1],
                                               in1=ps_c[:, P:2 * P], op0=ALU.mult,
                                               op1=ALU.add).then_inc(state_ready, 1)

            def ret_stats(p, c):
                dve.wait_ge(o_copied, CHUNKS * p + c + 1)
                nc.vector.bn_stats(bn[:, c, :], o_ret[:, c, :]).then_inc(bn_done, 1)
                wait_apart(dve, bn_done, CHUNKS * p + c + 1)
                nc.vector.bn_aggr(mv[:, c, :], bn[:, c, :]).then_inc(aggr_done, 1)

            def ret_var(p, sec):
                cs = slice(PER_SEC * sec, PER_SEC * (sec + 1))
                dve.wait_ge(aggr_done, CHUNKS * p + PER_SEC * (sec + 1))
                nc.vector.tensor_scalar(zvar[:, cs], mv[:, cs, 1], ca[:, H_XI2:H_XI2 + 1], EPS, ALU.mult,
                                        ALU.add).then_inc(var_ready, 1)

            def ret_norm(p, sec):
                cs = slice(PER_SEC * sec, PER_SEC * (sec + 1))
                dve.wait_ge(rvar_ready, nth(p, sec))
                nc.vector.tensor_scalar(rscale[:, cs], rvar[:, cs], ca[:, H_XIH:H_XIH + 1], None,
                                        ALU.mult).then_inc(scale_ready, 1)
                dve.wait_ge(scale_ready, nth(p, sec))
                for c in range(PER_SEC * sec, PER_SEC * (sec + 1)):
                    last = nc.vector.tensor_scalar(o_ret[:, c, :], o_ret[:, c, :], mv[:, c, 0:1],
                                                   rscale[:, c:c + 1], ALU.subtract, ALU.mult)
                last.then_inc(o_normed, 1)

            def att_bias(p, t, b):
                dve.wait_ge(att_scored, CHUNKS * p + b + 1)
                lo = P if t == 0 and b == 0 else 0
                par = b % 2
                nc.vector.tensor_copy(score[:, par, :, KEYS], sink[:, :])
                for h, bank in ((0, ps_a), (1, ps_b)):
                    last = nc.vector.tensor_tensor_reduce(score[:, par, h, lo:KEYS], bank[:, lo:KEYS],
                                                          bias[:, h, lo:KEYS], 1.0, sink[:, h:h + 1], ALU.add,
                                                          ALU.max, top[:, par, h:h + 1])
                last.then_inc(att_biased, 1)
                dve.wait_ge(att_biased, CHUNKS * p + b + 1)
                nc.vector.tensor_scalar(ntop[:, par, :], top[:, par, :], -1.0, None,
                                        ALU.mult).then_inc(max_ready, 1)

            def att_scale(p, b):
                par = b % 4
                dve.wait_ge(exp_done, CHUNKS * p + b + 1)
                nc.vector.reciprocal(rsum[:, par, :], esum[:, par, :]).then_inc(rsum_ready, 1)
                dve.wait_ge(att_summed, CHUNKS * p + b + 1)
                dve.wait_ge(rsum_ready, CHUNKS * p + b + 1)
                nc.vector.scalar_tensor_tensor(
                    out=o_att[:, :].rearrange("p (h d) -> p h d", h=2),
                    in0=ps_e[:, 0:P].rearrange("p (h d) -> p h d", h=2), scalar=0.5,
                    in1=rsum[:, par, :].unsqueeze(2).to_broadcast([P, 2, 64]),
                    op0=ALU.mult, op1=ALU.mult).then_inc(oatt_scaled, 1)

            def att_start(p, j):
                nc.vector.tensor_copy(cb[:, :], cst[:, bass.ds(C_HEAD + N_HEAD * j, N_HEAD)]).then_inc(att_consts, 1)
                nc.vector.tensor_copy(sink[:, :], sink_all[:, :, bass.ds(j, 1)]).then_inc(att_consts, 1)
                dve.wait_ge(att_consts, 2 * p + 2)
                for h in range(2):
                    nc.vector.tensor_scalar(bias[:, h, :], cst[:, C_DIST:C_DIST + KEYS],
                                            cb[:, H_SLOPE + h:H_SLOPE + h + 1], None,
                                            ALU.mult).then_inc(bias_made, 1)
                dve.wait_ge(bias_made, 2 * p + 2)

            def att_steps(p, t, s):
                if s == 8:
                    combine("ag", p, 0)
                if 0 <= s - 3 < CHUNKS:
                    att_scale(p, s - 3)
                if s < CHUNKS:
                    att_bias(p, t, s)

            def phase_a(t, j, x_tiles):
                ph = Phase("A", t, j)
                p = ph.p
                nc.vector.tensor_copy(ca[:, :], cst[:, bass.ds(C_HEAD + N_HEAD * j, N_HEAD)]).then_inc(ret_consts, 1)
                load_state(t, j, p)
                dve.wait_ge(ret_consts, p + 1)
                for s in range(12):
                    if s == 4:
                        make_gate("rg", p, 0)
                    if s == 6:
                        make_gate("ag", p, 0)
                    if s == 10:
                        make_gate("rg", p, 1)
                    if 0 <= s - 1 < CHUNKS:
                        ret_state(p, s - 1)
                    if s < CHUNKS:
                        ret_mask(p, s)
                    if 0 <= s - 1 < CHUNKS:
                        ret_stats(p, s - 1)
                    if s == 4:
                        ret_var(p, 0)
                    if s == 5:
                        ret_norm(p, 0)
                    if s == 8:
                        ret_var(p, 1)
                        dve.wait_ge(state_ready, (CHUNKS + 1) * (p + 1))
                        combine("rg", p, 0)
                        nc.vector.tensor_copy(state_all[:, bass.ds(j, 1), :], state[:, :]).then_inc(state_saved, 1)
                    if s == 9:
                        ret_norm(p, 1)
                        att_start(p, j)
                    if s in x_tiles:
                        x_low(x_tiles[s])
                make_gate("ag", p, 1)
                combine("rg", p, 1)

            def phase_b(att_t, att_p):
                if att_p is None:
                    for i in range(4, 8):
                        x_low(i)
                        if i + 2 < 8:
                            x_norm(i + 2)
                    for i in range(8, 12):
                        x_norm(i)
                    for i in range(8, 12):
                        x_low(i)
                    for i in range(12, 16):
                        x_norm(i)
                    return
                for s in range(12):
                    att_steps(att_p, att_t, s)
                combine("ag", att_p, 1)

            dve.wait_ge(gain_in, 16)
            x_norm(0)
            x_norm(1)
            for i in range(4):
                x_low(i)
                x_norm(i + 2)
            dve.wait_ge(const_in, 32)
            for t in range(2):
                phase_b(0, None if t == 0 else 3)
                with dve.Fori(0, HEADS - 1) as j:
                    phase_a(t, j, {})
                    phase_b(t, 4 * t + j)
                phase_a(t, 3, {6: 12, 7: 13, 8: 14, 9: 15} if t == 0 else {})

            def w_out_low(q):
                w = IN_GROUPS + q
                hi, lo = w_out_parts(q)
                dve.wait_ge(w_hi, w + 1)
                nc.vector.tensor_tensor(lo, wraw[:, w % 2, :, :], hi, ALU.subtract).then_inc(w_out_ready, 1)

            def out_gain(n):
                i, c = out_units[n]
                cols = slice(SEC * c, SEC * (c + 1))
                dve.wait_ge(out_squared, n + 1)
                if i >= 2 and c == 0:
                    dve.wait_ge(out_stored[i % 2], 16 * (i // 2))
                nc.vector.tensor_tensor(out_sb[i % 2][:, cols], out_banks[n % 3][:, :], gain[:, cols],
                                        ALU.mult).then_inc(out_copied, 1)

            def out_finish(i):
                b, o = i % 2, out_sb[i % 2]
                n = tile_done(i) - 1
                dve.wait_ge(out_squared, n + 1)
                nc.vector.tensor_tensor(xss[:, b, 0:1], xss[:, b, 0:1], xss[:, b, 1:2],
                                        ALU.add).then_inc(out_ms, 1)
                dve.wait_ge(out_ms, i + 1)
                nc.vector.tensor_scalar(xz[:, b:b + 1], xss[:, b, 0:1], 1.0 / DM, EPS, ALU.mult,
                                        ALU.add).then_inc(out_var, 1)
                out_gain(n)
                dve.wait_ge(out_rs, i + 1)
                dve.wait_ge(out_copied, n + 1)
                dve.wait_ge(res_in[i % 4], 16 * (i // 4 + 1))
                parts = [slice(0, DM)] if i < TILES - 1 else [slice(0, SEC), slice(SEC, DM)]
                for cols in parts:
                    nc.vector.scalar_tensor_tensor(out=o[:, cols], in0=o[:, cols], scalar=xr[:, b:b + 1],
                                                   in1=xt[:, i % 4, cols], op0=ALU.mult,
                                                   op1=ALU.add).then_inc(out_added, 1)

            def out_unit(n):
                if out_units[n][1] == 1:
                    out_finish(out_units[n][0])
                else:
                    out_gain(n)

            dve.wait_ge(gain_in, 32)
            for s in range(12):
                att_steps(7, 1, s)
                if s == 0:
                    w_out_low(4)
                    w_out_low(5)
                if s >= 2 and s % 2 == 0:
                    out_unit(s // 2 - 1)
                if s in (2, 3):
                    w_out_low(4 + s)
            combine("ag", 7, 1)
            for n in range(5, 2 * TILES):
                out_unit(n)

def shape_constants():
    import numpy as np

    c = np.zeros((P, C_ALL), np.float64)
    i = np.arange(P)
    c[:, C_MASK:C_MASK + P] = i[:, None] <= i[None, :]
    dist = i[:, None] + P - np.arange(KEYS)[None, :]
    c[:, C_DIST:C_DIST + KEYS] = np.where((dist >= 0) & (dist < P), -dist, -1e33)
    for j in range(HEADS):
        h = c[:, C_HEAD + N_HEAD * j:C_HEAD + N_HEAD * (j + 1)]
        decay = 1.0 - 2.0 ** (-5.0 - j)
        h[:, H_SLOPE] = 2.0 ** -(j + 1.0)
        h[:, H_SLOPE + 1] = 2.0 ** -(j + 5.0)
        h[:, H_GCINV] = decay ** -float(P)
        h[:, H_GC] = decay ** float(P)
        h[:, H_XI2] = decay ** (2.0 * (i + 1))
        h[:, H_XIH] = 0.5 * decay ** (i + 1.0)
        h[:, H_ZETA] = decay ** (P - 1.0 - i) * P ** -0.5
    return c.astype(np.float32)


def kernel(x, g_pre, w_in, sinks, w_out, g_post):
    import numpy as np
    import concourse.bacc as bacc
    from concourse.bass_utils import run_bass_kernel_spmd

    nc = bacc.Bacc("TRN2", target_bir_lowering=False, num_devices=1)
    arrays = {"x": np.ascontiguousarray(x).reshape(SEQ, DM), "g_pre": np.ascontiguousarray(g_pre),
              "w_in": np.ascontiguousarray(w_in), "sinks": np.ascontiguousarray(sinks),
              "w_out": np.ascontiguousarray(w_out), "g_post": np.ascontiguousarray(g_post),
              "consts": shape_constants()}
    args = [nc.dram_tensor(n, a.shape, F32, kind="ExternalInput").ap() for n, a in arrays.items()]
    mix = nc.dram_tensor("mix", (TILES, P, 2 * HEADS, P), F32, kind="Internal").ap()
    out = nc.dram_tensor("out", (SEQ, DM), F32, kind="ExternalOutput").ap()
    hybrid_layer(nc, *args, mix, out)
    r = run_bass_kernel_spmd(nc, [arrays], core_ids=[0])
    return r.results[0]["out"].reshape(1, SEQ, DM)
```

```python
from contextlib import ExitStack

import concourse.bass as bass
from concourse import mybir

F32 = mybir.dt.float32
F32R = mybir.dt.float32r
ALU = mybir.AluOpType
ACT = mybir.ActivationFunctionType

P = 128
SEQ = 2048
DM = 1024
KT = DM // P
SEC = 512
HALF = 1024
HEADS = 4
CHUNKS = HALF // P
PER_SEC = SEC // P
TILES = SEQ // P
EPS = 1e-6
KEYS = 2 * P

COL = {"rq": 0, "rk": 512, "rv": 1024, "rg": 1536, "aq": 2048, "ak": 2560, "av": 2688, "ag": 2816}
A_UNITS = [("aq", 0), ("rg", 0), ("ag", 0), ("aq", 1), ("rg", 1), ("ag", 1)]
B_UNITS = [("rk", 0), ("rv", 0), ("rq", 0), ("rk", 1), ("rv", 1), ("rq", 1)]
K_UNITS = [("ak", 0), ("av", 0), ("ak", 1), ("av", 1)]
GROUPS = {"A": ["aq", "rg", "ag"], "B": ["rk", "rv", "rq"], "K": ["ak", "av"]}
HALF_GROUPS = 3 + 2 + 6 * HEADS - 3
HALF_UNITS = 2 * HALF_GROUPS
IN_GROUPS = 2 * HALF_GROUPS
OUT_CHUNKS = DM // P

C_MASK, C_DIST, C_HEAD, N_HEAD = 0, 2 * P, 2 * P + KEYS, 8
C_ALL = C_HEAD + HEADS * N_HEAD
H_SLOPE, H_GCINV2, H_GC, H_XI2, H_XIH, H_ZETA = 0, 2, 3, 4, 5, 6


def wait_apart(eng, sem, count):
    if not isinstance(count, int):
        eng.wait_ge(sem, 1)
    eng.wait_ge(sem, count)


class Phase:

    def __init__(self, kind, t, j):
        self.kind, self.t, self.j = kind, t, j
        self.p = 4 * t + j
        self.groups = GROUPS[kind]
        self.n = len(self.groups)
        first = isinstance(j, int) and j == 0 and kind == "B"
        base = {"A": 5, "B": 0 if first else 2, "K": 3}[kind] + HALF_GROUPS * t
        steps = 0 if kind == "K" or first else j
        self.w0, self.w = base, base + 6 * steps
        self.u = 2 * base + 12 * steps

    def slot(self, g):
        return (self.w0 + g) % 3

    def group_used(self, g):
        return self.u + self.n + g + 1


def nth(p, sec):
    return 2 * p + sec + 1


def hybrid_layer(nc, x, g_pre, w_in, sinks, w_out, g_post, consts, mix, out):
    ctx = ExitStack()
    with ctx:
        def sb(name, shape, dt=F32):
            return ctx.enter_context(nc.sbuf_tensor(name, shape, dt))

        def sem(name):
            return ctx.enter_context(nc.semaphore(name))

        cst = sb("cst", [P, C_ALL])
        ident = sb("ident", [P, P])
        gain = sb("gain", [P, DM])
        sink_all = sb("sink_all", [P, 2, HEADS])
        big = sb("big", [P, 3, 2, KT, SEC], F32R)
        wslot = sb("wslot", [P, 3, 2, KT, P], F32R)
        wraw = sb("wraw", [P, KT, P])
        xt = sb("xt", [P, 4, DM])
        rk_t = sb("rk_t", [P, HALF])
        rv_t = sb("rv_t", [P, HALF])
        rq_t = sb("rq_t", [P, HALF])
        aq_s = sb("aq_s", [P, 2, HALF], F32R)
        gate = {"rg": sb("rgate", [P, HALF]), "ag": sb("agate", [P, HALF])}
        k_nat, v_nat, p_ret = [gain[:, 2 * P * i:2 * P * (i + 1)].rearrange("p (a n) -> p a n", a=2)
                               for i in range(3)]
        state = gain[:, 6 * P:7 * P]
        state_all = sb("state_all", [P, HEADS, P])
        o_ret = sb("o_ret", [P, CHUNKS, P])
        ak_s = sb("ak_s", [P, 2, (CHUNKS + 1) * P], F32R)
        ak_lo = sb("ak_lo", [P, (CHUNKS + 1) * P], F32R)
        av_n = sb("av_n", [P, CHUNKS + 1, P])
        bias = sb("bias", [P, 2, KEYS])
        biased = sb("biased", [P, 2, KEYS])
        score = sb("score", [P, 2, 2, P + 1])
        p_t = sb("p_t", [P, 2, 2, P])
        ca = sb("ca", [P, N_HEAD])
        cb = sb("cb", [P, N_HEAD])
        cz = sb("cz", [P, 1])
        sink = sb("sink", [P, 2])
        bn = sb("bn", [P, CHUNKS, 6])
        mv = sb("mv", [P, CHUNKS, 2])
        zvar = sb("zvar", [P, CHUNKS])
        rvar = sb("rvar", [P, CHUNKS])
        rscale = sb("rscale", [P, CHUNKS])
        minus_half = sb("minus_half", [P, PER_SEC])
        top = sb("top", [P, 2, 2])
        ntop = sb("ntop", [P, 2, 2])
        esum = sb("esum", [P, 2, 2])
        rsum = sb("rsum", [P, 2, 2])
        xss = sb("xss", [P, 2, 2])
        xz = sb("xz", [P, 2])
        xr = sb("xr", [P, 2])
        credit = sb("credit", [P, 4])

        proj = [ctx.enter_context(nc.psum_tensor(f"proj{i}", [P, SEC], F32)) for i in range(2)]
        ps_a, ps_b, ps_c, ps_d, ps_e, ps_f = [
            ctx.enter_context(nc.psum_tensor(f"ps_{i}", [P, SEC], F32)) for i in "abcdef"]

        const_in = sem("const_in")
        gain_in = sem("gain_in")
        ident_made = sem("ident_made")
        halves_made = sem("halves_made")
        x_in = [sem(f"x_in{i}") for i in range(4)]
        x_squared = sem("x_squared")
        x_var = sem("x_var")
        x_rs = sem("x_rs")
        x_normed = sem("x_normed")
        x_turned = sem("x_turned")
        x_hi = sem("x_hi")
        x_lo = sem("x_lo")
        raw_in = sem("raw_in")
        first_in = sem("first_in")
        w_out_in = [sem(f"w_out_in{i}") for i in range(2)]
        w_hi = sem("w_hi")
        w_ready = sem("w_ready")
        w_out_ready = sem("w_out_ready")
        unit_done = sem("unit_done")
        copied = {k: sem(f"copied_{k}") for k in ("rk", "rv", "rq", "aq", "ak", "av")}
        tanh_done = {k: sem(f"tanh_{k}") for k in ("rg", "ag")}
        gated = {k: sem(f"gated_{k}") for k in ("rg", "ag")}
        aq_hi = sem("aq_hi")
        ak_hi = sem("ak_hi")
        v_turned = sem("v_turned")
        v_kept = sem("v_kept")
        ret_consts = sem("ret_consts")
        zeta_here = sem("zeta_here")
        ret_scored = sem("ret_scored")
        kv_copied = sem("kv_copied")
        ret_masked = sem("ret_masked")
        ret_summed = sem("ret_summed")
        o_copied = sem("o_copied")
        state_ready = sem("state_ready")
        state_saved = sem("state_saved")
        bn_done = sem("bn_done")
        aggr_done = sem("aggr_done")
        var_ready = sem("var_ready")
        rvar_ready = sem("rvar_ready")
        scale_ready = sem("scale_ready")
        o_normed = sem("o_normed")
        ret_turned = sem("ret_turned")
        combined = {k: sem(f"combined_{k}") for k in ("rg", "ag")}
        stored = {k: [sem(f"stored_{k}{i}") for i in range(2)] for k in ("rg", "ag")}
        att_consts = sem("att_consts")
        bias_made = sem("bias_made")
        att_scored = sem("att_scored")
        att_biased = sem("att_biased")
        max_ready = sem("max_ready")
        exp_done = sem("exp_done")
        p_turned = sem("p_turned")
        p_masked = sem("p_masked")
        p_scaled = sem("p_scaled")
        rsum_ready = sem("rsum_ready")
        att_summed = sem("att_summed")
        mix_in = [sem(f"mix_in{i}") for i in range(2)]
        mix_hi = sem("mix_hi")
        mix_ready = sem("mix_ready")
        res_in = [sem(f"res_in{i}") for i in range(4)]
        out_done = sem("out_done")
        out_squared = sem("out_squared")
        out_copied = sem("out_copied")
        out_ms = sem("out_ms")
        out_var = sem("out_var")
        out_rs = sem("out_rs")
        out_added = sem("out_added")
        out_stored = [sem(f"out_stored{i}") for i in range(2)]

        w_in_v = w_in.rearrange("(k p) c -> p k c", p=P)
        w_out_v = w_out.rearrange("(k p) c -> p k c", p=P)
        w_out_pair = w_out[4 * P:, :].rearrange("(h k q) c -> h q k c", h=2, k=HEADS)
        n_tok = {"rg": 0, "ag": HEADS}

        masks = cst[:, C_MASK:C_MASK + 2 * P].rearrange("p (e n) -> p e n", e=2)
        turned = [ps_d, ps_e]

        def hbuf(t, sec):
            return (2 * t + sec) % 3

        o_flat = o_ret[:, :, :].rearrange("p c d -> p (c d)")
        mix_raw = [rk_t[:, :], rv_t[:, :]]
        out_sb = [rq_t[:, :], o_flat]
        x_junk = o_flat
        out_junk = state_all[:, :, :].rearrange("p h d -> p (h d)")

        def as_group(tile):
            return tile.rearrange("p (k n) -> p k n", n=P)

        first_raw = [wraw[:, :, :], as_group(gate["rg"][:, :]), as_group(gate["ag"][:, :])]
        head_rows = [slice(0, 64), slice(64, P)]

        def mix_split(i, part):
            return big[:, 2, part, :, P * (i % 4):P * (i % 4) + P]

        def w_out_at(c):
            return 1 if c == 0 else 0

        def w_out_raw(q):
            return as_group(xt[:, q % 4, :])

        def w_out_parts(q):
            cols = slice(P * (q % 4), P * (q % 4) + P)
            return [big[:, w_out_at(q // 4), part, :, cols] for part in range(2)]

        def x_banks(i):
            return (ps_c, ps_d) if i < 12 and i % 2 == 0 else (ps_e, ps_f)

        out_units = [(0, 0), (1, 0), (0, 1), (1, 1)] + [(i, c) for i in range(2, TILES) for c in range(2)]
        out_banks = [proj[0], proj[1], ps_f]

        def tile_done(i):
            return out_units.index((i, 1)) + 1

        block = ctx.enter_context(nc.Block())

        @block.sync
        def _(sp):
            def load_w(ph, g):
                kind, j = ph.groups[g], ph.j
                dst, loaded = wraw[:, :, :], raw_in
                if ph.kind == "B" and isinstance(ph.w, int) and ph.w == 0:
                    dst, loaded = first_raw[g], first_in if g else raw_in
                else:
                    sp.wait_ge(w_ready, ph.w + g)
                if kind in ("aq", "ag"):
                    for h in range(2):
                        src = w_in_v[:, :, bass.ds(COL[kind] + 256 * h + 64 * j, 64)]
                        sp.dma_start(dst[:, :, 64 * h:64 * h + 64], src).then_inc(loaded, 16)
                else:
                    col = COL[kind] if kind in ("ak", "av") else COL[kind] + P * j
                    for h in (1, 0):
                        src = w_in_v[:, 4 * h:4 * h + 4, bass.ds(col, P)]
                        sp.dma_start(dst[:, 4 * h:4 * h + 4, :], src).then_inc(loaded, 16)

            def load_x(i):
                if i >= 4:
                    sp.wait_ge(x_turned, i - 3)
                sp.dma_start(xt[:, i % 4, :], x[i * P:(i + 1) * P, :]).then_inc(x_in[i % 4], 16)

            def store(kind, t, j, sec):
                sp.wait_ge(combined[kind], nth(4 * t + j, sec))
                tile = PER_SEC * (2 * t + sec)
                dst = mix[tile:tile + PER_SEC, :, bass.ds(n_tok[kind] + j, 1), :]
                sp.dma_start(dst.rearrange("i p g n -> p (i g) n"),
                             gate[kind][:, SEC * sec:SEC * (sec + 1)].rearrange("p (i n) -> p i n", n=P)
                             ).then_inc(stored[kind][sec], 16)

            def load_w_out(q):
                c, dst = q // 4, w_out_raw(q)
                if q >= 4:
                    sp.wait_ge(w_ready, IN_GROUPS + q - 3)
                cols = slice(q * P, (q + 1) * P)
                sp.dma_start(dst[:, 0:4, :], w_out_v[:, 0:4, cols]).then_inc(w_out_in[c], 16)
                for h in range(2):
                    sp.dma_start(dst[64 * h:64 * h + 64, 4:8, :],
                                 w_out_pair[h, :, :, cols]).then_inc(w_out_in[c], 16)

            first = Phase("B", 0, 0)
            load_x(0)
            sp.dma_start(gain[:, :], g_pre.partition_broadcast(P)).then_inc(gain_in, 16)
            load_x(1)
            load_x(2)
            load_x(3)
            load_w(first, 0)
            load_x(4)
            load_x(5)
            load_w(first, 1)
            load_x(6)
            sp.dma_start(cst[:, :], consts).then_inc(const_in, 16)
            sp.dma_start(sink_all[:, :, :].rearrange("p a b -> p (a b)"),
                         sinks.partition_broadcast(P)).then_inc(const_in, 16)
            load_w(first, 2)
            load_x(7)
            for t in range(2):
                nxt = Phase("K", t, 0)
                if t == 0:
                    for i in range(8, 12):
                        load_x(i)
                load_w(nxt, 0)
                if t == 1:
                    store("ag", 0, 3, 0)
                load_w(nxt, 1)
                nxt = Phase("A", t, 0)
                for g in range(3):
                    load_w(nxt, g)
                    if t == 0 and g < 2:
                        load_x(12 + 2 * g)
                        load_x(13 + 2 * g)
                    if t == 1 and g == 0:
                        store("ag", 0, 3, 1)
                with sp.Fori(0, HEADS - 1) as j:
                    nxt = Phase("B", t, j + 1)
                    load_w(nxt, 0)
                    store("rg", t, j, 0)
                    load_w(nxt, 1)
                    load_w(nxt, 2)
                    store("rg", t, j, 1)
                    nxt = Phase("A", t, j + 1)
                    load_w(nxt, 0)
                    store("ag", t, j, 0)
                    load_w(nxt, 1)
                    load_w(nxt, 2)
                    store("ag", t, j, 1)
                if t == 0:
                    nxt = Phase("B", 1, 0)
                    load_w(nxt, 0)
                    store("rg", 0, 3, 0)
                    load_w(nxt, 1)
                    load_w(nxt, 2)
                    store("rg", 0, 3, 1)

            def load_mix(i):
                if i >= 2:
                    sp.wait_ge(mix_ready, i - 1)
                else:
                    sp.wait_ge(ret_summed, 8 * CHUNKS)
                sp.dma_start(mix_raw[i % 2].rearrange("p (g n) -> p g n", n=P),
                             mix[i, :, :, :]).then_inc(mix_in[i % 2], 16)

            def load_res(i):
                if i >= 4:
                    sp.wait_ge(out_added, i - 3)
                else:
                    sp.wait_ge(w_out_ready, i + 1)
                sp.dma_start(xt[:, i % 4, :], x[i * P:(i + 1) * P, :]).then_inc(res_in[i % 4], 16)

            def store_out(i):
                if i < TILES - 1:
                    sp.wait_ge(out_added, i + 1)
                    sp.dma_start(out[i * P:(i + 1) * P, :], out_sb[i % 2]).then_inc(out_stored[i % 2], 16)
                    return
                for c in range(2):
                    cols = slice(SEC * c, SEC * (c + 1))
                    sp.wait_ge(out_added, i + c + 1)
                    sp.dma_start(out[i * P:(i + 1) * P, cols], out_sb[i % 2][:, cols]
                                 ).then_inc(out_stored[i % 2], 16)

            sp.wait_ge(x_turned, TILES)
            for q in range(8):
                load_w_out(q)
            store("rg", 1, 3, 0)
            for sec in range(2):
                for k in ("rg", "ag"):
                    sp.wait_ge(stored[k][sec], 16 * (HEADS + 1))
            load_mix(0)
            load_mix(1)
            sp.wait_ge(ret_turned, nth(7, 1))
            sp.dma_start(gain[:, :], g_post.partition_broadcast(P)).then_inc(gain_in, 16)
            store("rg", 1, 3, 1)
            load_mix(2)
            load_res(0)
            load_res(1)
            load_mix(3)
            load_res(2)
            for i in range(TILES):
                if i + 4 < TILES:
                    if i + 4 == TILES // 2:
                        for sec in range(2):
                            for k in ("rg", "ag"):
                                sp.wait_ge(stored[k][sec], 16 * (2 * HEADS + 1))
                    load_mix(i + 4)
                store_out(i)
                if i + 3 < TILES:
                    load_res(i + 3)
                if i in (1, 2):
                    store("ag", 1, 3, i - 1)
            sp.wait_ge(out_stored[0], 16 * TILES // 2)
            sp.wait_ge(out_stored[1], 16 * (TILES // 2 + 1))

        @block.gpsimd
        def _(pool):
            nc.gpsimd.memset(minus_half[:, :], -0.5).then_inc(halves_made, 1)
            nc.gpsimd.memset(ident[:, :], 0.0).then_inc(ident_made, 1)
            pool.wait_ge(ident_made, 1)
            nc.gpsimd.affine_select(out=ident[:, :], in_=ident[:, :], compare_op=ALU.not_equal, fill=1.0,
                                    base=0, pattern=[[-1, P]], channel_multiplier=1).then_inc(ident_made, 1)

            def split_low(ph, g):
                raw = first_raw[g] if ph.kind == "B" and isinstance(ph.w, int) and ph.w == 0 else wraw[:, :, :]
                pool.wait_ge(w_hi, ph.w + g + 1)
                nc.gpsimd.tensor_tensor(wslot[:, ph.slot(g), 1, :, :], raw, wslot[:, ph.slot(g), 0, :, :],
                                        ALU.subtract).then_inc(w_ready, 1)

            def x_power(i):
                pool.wait_ge(x_var, i + 1)
                nc.gpsimd.tensor_tensor(xr[:, i % 2:i % 2 + 1], xz[:, i % 2:i % 2 + 1],
                                        minus_half[:, 0:1], ALU.pow).then_inc(x_rs, 1)

            def ret_power(p, sec):
                pool.wait_ge(var_ready, nth(p, sec))
                cs = slice(PER_SEC * sec, PER_SEC * (sec + 1))
                nc.gpsimd.tensor_tensor(rvar[:, cs], zvar[:, cs], minus_half[:, :],
                                        ALU.pow).then_inc(rvar_ready, 1)

            pool.wait_ge(halves_made, 1)
            first = Phase("B", 0, 0)
            for i in range(4):
                x_power(i)
            for g in range(3):
                split_low(first, g)
                for i in ((4,), (5, 6), (7,))[g]:
                    x_power(i)
            for i in range(8, 12):
                x_power(i)
            for t in range(2):
                nxt = Phase("K", t, 0)
                for g in range(2):
                    split_low(nxt, g)
                nxt = Phase("A", t, 0)
                split_low(nxt, 0)
                if t == 0:
                    for i in range(12, 16):
                        x_power(i)
                split_low(nxt, 1)
                split_low(nxt, 2)
                with pool.Fori(0, HEADS - 1) as j:
                    p, nxt = 4 * t + j, Phase("B", t, j + 1)
                    ret_power(p, 0)
                    split_low(nxt, 0)
                    ret_power(p, 1)
                    split_low(nxt, 1)
                    split_low(nxt, 2)
                    nxt = Phase("A", t, j + 1)
                    for g in range(3):
                        split_low(nxt, g)
                if t == 0:
                    nxt = Phase("B", 1, 0)
                    ret_power(3, 0)
                    split_low(nxt, 0)
                    ret_power(3, 1)
                    split_low(nxt, 1)
                    split_low(nxt, 2)

            def split_w_out_low(q):
                hi, lo = w_out_parts(q)
                pool.wait_ge(w_hi, IN_GROUPS + q + 1)
                nc.gpsimd.tensor_tensor(lo, w_out_raw(q), hi, ALU.subtract).then_inc(w_ready, 1)

            def split_mix_low(i):
                pool.wait_ge(mix_hi, i + 1)
                nc.gpsimd.tensor_tensor(mix_split(i, 1), mix_raw[i % 2].rearrange("p (g n) -> p g n", n=P),
                                        mix_split(i, 0), ALU.subtract).then_inc(mix_ready, 1)

            def out_power(i):
                pool.wait_ge(out_var, i + 1)
                nc.gpsimd.tensor_tensor(xr[:, i % 2:i % 2 + 1], xz[:, i % 2:i % 2 + 1],
                                        minus_half[:, 0:1], ALU.pow).then_inc(out_rs, 1)

            for q in range(4):
                split_w_out_low(q)
                if q in (1, 3):
                    ret_power(7, q // 2)
            for i in range(3):
                split_mix_low(i)
            for i in range(TILES):
                out_power(i)
                if i + 3 < TILES:
                    split_mix_low(i + 3)

        @block.tensor
        def _(pe):
            def turn_x(i):
                pe.wait_ge(x_normed, i + 1)
                if i >= 12:
                    pe.wait_ge(x_lo, 2 * i)
                elif i >= 2:
                    pe.wait_ge(x_lo, 2 * (i - 1))
                for k in range(KT):
                    last = nc.tensor.transpose(x_banks(i)[k // 4][:, P * (k % 4):P * (k % 4) + P],
                                               xt[:, i % 4, P * k:P * (k + 1)], ident[:, :])
                last.then_inc(x_turned, 1)

            def unit_half(ph, units, s, bank_free):
                u, half = divmod(s, 2)
                kind, sec = units[u]
                g = ph.groups.index(kind)
                if half == 0:
                    if bank_free is not None:
                        pe.wait_ge(*bank_free)
                    if sec == 0:
                        pe.wait_ge(w_ready, ph.w + g + 1)
                w, h = ph.slot(g), hbuf(ph.t, sec)
                bank = proj[u % 2]
                for k in range(4 * half, 4 * half + 4):
                    for wp, hp in ((0, 0), (0, 1), (1, 0)):
                        last = nc.tensor.matmul(bank[:, :], wslot[:, w, wp, k, :], big[:, h, hp, k, :],
                                                start=(k == 0 and wp + hp == 0), stop=(k == KT - 1 and wp == 1))
                if half == 1:
                    last.then_inc(unit_done, 1)

            def first_unit_part(ph, part):
                pe.wait_ge(x_lo, 4 * (part + 1))
                if part == 0:
                    pe.wait_ge(w_ready, 1)
                cols = slice(SEC // 2 * part, SEC // 2 * (part + 1))
                for k in range(KT):
                    for wp, hp in ((0, 0), (0, 1), (1, 0)):
                        last = nc.tensor.matmul(proj[0][:, cols], wslot[:, ph.slot(0), wp, k, :],
                                                big[:, 0, hp, k, cols],
                                                start=(k == 0 and wp + hp == 0), stop=(k == KT - 1 and wp == 1))
                if part == 1:
                    last.then_inc(unit_done, 1)

            def evacuated(kind, sec, p):
                return (gated if kind in gated else copied)[kind], nth(p, sec)

            def ret_score(p, c):
                sec, par = c // PER_SEC, slice(c * P, (c + 1) * P)
                if c % PER_SEC == 0:
                    for k in ("rk", "rv", "rq"):
                        pe.wait_ge(copied[k], nth(p, sec))
                nc.tensor.transpose(ps_a[:, 0:P], rk_t[:, par], ident[:, :])
                nc.tensor.transpose(ps_a[:, P:2 * P], rv_t[:, par], ident[:, :])
                nc.tensor.matmul(ps_b[:, 0:P], rk_t[:, par], rq_t[:, par],
                                 start=True, stop=True).then_inc(ret_scored, 1)

            def ret_sum(p, c):
                n = CHUNKS * p + c
                pe.wait_ge(kv_copied, n + 1)
                pe.wait_ge(ret_masked, n + 1)
                pe.wait_ge(state_ready, (CHUNKS + 1) * p + c + 1)
                nc.tensor.matmul(ps_c[:, P:2 * P], k_nat[:, c % 2, :], v_nat[:, c % 2, :], start=True, stop=True)
                nc.tensor.matmul(ps_c[:, 0:P], p_ret[:, c % 2, :], v_nat[:, c % 2, :], start=True, stop=False)
                nc.tensor.matmul(ps_c[:, 0:P], rq_t[:, c * P:(c + 1) * P], state[:, :],
                                 start=False, stop=True).then_inc(ret_summed, 1)

            def ret_turn(p, sec):
                pe.wait_ge(o_normed, nth(p, sec))
                for c in range(PER_SEC):
                    last = nc.tensor.transpose(turned[sec][:, c * P:(c + 1) * P], o_ret[:, PER_SEC * sec + c, :],
                                               ident[:, :])
                last.then_inc(ret_turned, 1)

            def att_score(p, t, b):
                if b % PER_SEC == 0:
                    pe.wait_ge(copied["aq"], nth(p, b // PER_SEC))
                    pe.wait_ge(copied["ak"], nth(t, 1))
                if b >= 1:
                    pe.wait_ge(att_biased, CHUNKS * p + b)
                lo = P if t == 0 and b == 0 else 0
                for h, bank in enumerate((ps_a, ps_b)):
                    nc.tensor.matmul(bank[:, lo:KEYS], aq_s[:, h, b * P:(b + 1) * P],
                                     ak_s[:, h, b * P + lo:b * P + KEYS], start=True, stop=False)
                for rows, h, bank in ((head_rows[0], 0, ps_a), (head_rows[1], 1, ps_b)):
                    last = nc.tensor.matmul(bank[:, lo:KEYS], aq_s[rows, h, b * P:(b + 1) * P],
                                            ak_lo[rows, b * P + lo:b * P + KEYS], start=False, stop=True)
                last.then_inc(att_scored, 1)

            def att_turn_p(p, b):
                pe.wait_ge(p_scaled, CHUNKS * p + b + 1)
                for h in range(2):
                    last = nc.tensor.transpose(ps_c[:, P * h:P * (h + 1)], score[:, b % 2, h, 0:P], ident[:, :])
                last.then_inc(p_turned, 1)

            def att_sum(p, t, b):
                pe.wait_ge(p_masked, CHUNKS * p + b + 1)
                if b == 0:
                    pe.wait_ge(v_kept, nth(t, 1))
                es = (1,) if t == 0 and b == 0 else (0, 1)
                for e in es:
                    for h, rows in enumerate(head_rows):
                        last = nc.tensor.matmul(turned[b // PER_SEC][rows, P * (b % PER_SEC):P * (b % PER_SEC + 1)],
                                                av_n[:, b + e, rows], p_t[:, h, e, :],
                                                start=(e == es[0]), stop=(e == 1))
                last.then_inc(att_summed, 1)

            def att_steps(p, t, s):
                if 0 <= s - 3 < CHUNKS:
                    att_sum(p, t, s - 3)
                if 0 <= s - 2 < CHUNKS:
                    att_turn_p(p, s - 2)
                if s < CHUNKS:
                    att_score(p, t, s)

            def phase_a(t, j, x_tiles):
                ph = Phase("A", t, j)
                for s in range(12):
                    if s == 7:
                        ret_turn(ph.p, 0)
                    if 0 <= s - 1 < CHUNKS:
                        ret_sum(ph.p, s - 1)
                    if s < CHUNKS:
                        ret_score(ph.p, s)
                    if s == 11:
                        if x_tiles:
                            pe.wait_ge(x_lo, 2 * TILES)
                        ret_turn(ph.p, 1)
                    if s in x_tiles:
                        turn_x(x_tiles[s])
                    u = s // 2
                    if u >= 2:
                        free = evacuated(*A_UNITS[u - 2], ph.p)
                    else:
                        free = evacuated(*B_UNITS[4 + u], ph.p)
                    unit_half(ph, A_UNITS, s, free)

            def phase_b(t, j, att_t, att_p):
                ph = Phase("B", t, j)
                for s in range(12):
                    if att_p is not None:
                        att_steps(att_p, att_t, s)
                    u = s // 2
                    if s in (0, 6) and isinstance(j, int) and j == 0 and (t, s) != (0, 0):
                        pe.wait_ge(x_lo, 2 * PER_SEC * (2 * t + s // 6 + 1))
                    if u >= 2:
                        free = evacuated(*B_UNITS[u - 2], ph.p)
                    elif att_p is not None:
                        free = evacuated(*A_UNITS[4 + u], att_p)
                    else:
                        free = None
                    if att_p is None and s < 2:
                        first_unit_part(ph, s)
                    else:
                        unit_half(ph, B_UNITS, s, free)
                    if att_p is None and s < 4:
                        turn_x(4 + s)

            def turn_v(t, sec):
                pe.wait_ge(copied["av"], nth(t, sec))
                if sec == 1:
                    pe.wait_ge(v_kept, nth(t, 0))
                for b in range(PER_SEC):
                    at = SEC * sec + P * b
                    last = nc.tensor.transpose(ps_f[:, P * b:P * (b + 1)], gate["rg"][:, at:at + P],
                                               ident[:, :])
                last.then_inc(v_turned, 1)

            def phase_k(t):
                ph = Phase("K", t, 0)
                for s in range(8):
                    if t == 0 and s < 4:
                        turn_x(8 + s)
                    if s == 5:
                        if t == 0:
                            pe.wait_ge(x_lo, 24)
                        turn_v(t, 0)
                    u = s // 2
                    free = evacuated(*K_UNITS[u - 2], t) if u >= 2 else evacuated(*B_UNITS[4 + u], ph.p)
                    unit_half(ph, K_UNITS, s, free)
                pe.wait_ge(copied["ak"], nth(t, 1))
                turn_v(t, 1)

            pe.wait_ge(ident_made, 2)
            for i in range(4):
                turn_x(i)
            for t in range(2):
                phase_b(t, 0, 0, None if t == 0 else 3)
                phase_k(t)
                with pe.Fori(0, HEADS - 1) as j:
                    phase_a(t, j, {})
                    phase_b(t, j + 1, t, 4 * t + j)
                phase_a(t, 3, {6: 12, 7: 13, 8: 14, 10: 15} if t == 0 else {})

            def out_half(n, half):
                i, c = out_units[n]
                bank = out_banks[n % 3]
                if half == 0:
                    if c == 0:
                        pe.wait_ge(mix_ready, i + 1)
                    if n < 2:
                        pe.wait_ge(*evacuated(*A_UNITS[4 + n], 7))
                    elif n == 2:
                        pe.wait_ge(v_kept, nth(1, 1))
                    else:
                        pe.wait_ge(out_copied, n - 2)
                    if n == 0:
                        pe.wait_ge(w_ready, IN_GROUPS + 4)
                    if n == 2:
                        pe.wait_ge(w_out_ready, 4)
                for k in range(4 * half, 4 * half + 4):
                    for mp, wp in ((0, 0), (0, 1), (1, 0)):
                        last = nc.tensor.matmul(bank[:, :], mix_split(i, mp)[:, k, :],
                                                big[:, w_out_at(c), wp, k, :],
                                                start=(k == 0 and mp + wp == 0), stop=(k == KT - 1 and mp == 1))
                if half == 1:
                    last.then_inc(out_done, 1)

            for n in range(2 * TILES):
                for half in range(2):
                    if 2 * n + half < 12:
                        att_steps(7, 1, 2 * n + half)
                    out_half(n, half)

        @block.scalar
        def _(act):
            def x_square(i):
                act.wait_ge(x_in[i % 4], 16 * (i // 4 + 1))
                if i >= 2:
                    act.wait_ge(x_var, i - 1)
                if i >= 1:
                    act.wait_ge(x_squared, i)
                nc.scalar.activation(x_junk, xt[:, i % 4, :], ACT.Square,
                                     accum_out=xss[:, i % 2, 0:1]).then_inc(x_squared, 1)

            def x_high(i):
                b, at = (i // PER_SEC) % 3, P * (i % PER_SEC)
                act.wait_ge(x_turned, i + 1)
                if i == 12:
                    act.wait_ge(unit_done, Phase("A", 0, 3).u + 3)
                for h, bank in enumerate(x_banks(i)):
                    nc.scalar.copy(big[:, b, 0, 4 * h:4 * h + 4, at:at + P],
                                   bank[:, :].rearrange("p (k n) -> p k n", n=P)).then_inc(x_hi, 1)

            def first_high(g):
                if g == 0:
                    act.wait_ge(raw_in, 32)
                else:
                    act.wait_ge(first_in, 64)
                nc.scalar.copy(wslot[:, g, 0, :, :], first_raw[g]).then_inc(w_hi, 1)

            def split_high(ph, g, used):
                act.wait_ge(raw_in, 32 * (ph.w + g) - 32)
                act.wait_ge(unit_done, used)
                nc.scalar.copy(wslot[:, ph.slot(g), 0, :, :], wraw[:, :, :]).then_inc(w_hi, 1)

            def w_out_high(q):
                act.wait_ge(w_out_in[q // 4], 4 * 48)
                if q == 4:
                    act.wait_ge(unit_done, 2 * HALF_UNITS)
                nc.scalar.copy(w_out_parts(q)[0], w_out_raw(q)).then_inc(w_hi, 1)

            def mix_high(i):
                act.wait_ge(mix_in[i % 2], 16 * (i // 2 + 1))
                if i >= 4:
                    act.wait_ge(out_done, tile_done(i - 4))
                elif i == 0:
                    act.wait_ge(unit_done, 2 * HALF_UNITS - 3)
                nc.scalar.copy(mix_split(i, 0), mix_raw[i % 2].rearrange("p (g n) -> p g n", n=P)
                               ).then_inc(mix_hi, 1)

            def after_a(t, j):
                if isinstance(j, int):
                    return Phase("B", 1, 0)
                return Phase("B", t, j + 1)

            def evacuate(ph, units, u):
                kind, sec = units[u]
                bank, cols = proj[u % 2], slice(SEC * sec, SEC * (sec + 1))
                act.wait_ge(unit_done, ph.u + u + 1)
                if kind in ("rg", "ag"):
                    act.wait_ge(stored[kind][sec], 16 * ph.p + 16)
                    nc.scalar.activation(gate[kind][:, cols], bank[:, :], ACT.Tanh,
                                         scale=0.5).then_inc(tanh_done[kind], 1)
                    return
                if kind == "aq":
                    for h, rows in enumerate(head_rows):
                        last = nc.scalar.activation(aq_s[rows, h, cols], bank[rows, :], ACT.Copy,
                                                    scale=0.125)
                    last.then_inc(aq_hi, 1)
                    return
                if kind == "ak":
                    cols = slice(P + SEC * sec, P + SEC * (sec + 1))
                    for h, rows in enumerate(head_rows):
                        for copy_rows in head_rows:
                            last = nc.scalar.copy(ak_s[copy_rows, h, cols], bank[rows, :])
                    last.then_inc(ak_hi, 1)
                    return
                if kind == "av":
                    act.wait_ge(stored["rg"][sec], 16 * ph.p + 16)
                dst = {"rk": rk_t, "rv": rv_t, "rq": rq_t, "av": gate["rg"]}[kind]
                nc.scalar.copy(dst[:, cols], bank[:, :]).then_inc(copied[kind], 1)

            def ret_copies(p, c):
                act.wait_ge(ret_scored, CHUNKS * p + c + 1)
                nc.scalar.copy(k_nat[:, c % 2, :], ps_a[:, 0:P])
                nc.scalar.activation(v_nat[:, c % 2, :], ps_a[:, P:2 * P], ACT.Copy,
                                     scale=cz[:, 0:1]).then_inc(kv_copied, 1)

            def att_exp(p, b):
                act.wait_ge(max_ready, CHUNKS * p + b + 1)
                for h in range(2):
                    c = score[:, b % 2, h, :]
                    last = nc.scalar.activation(c, c, ACT.Exp, bias=ntop[:, b % 2, h:h + 1],
                                                accum_out=esum[:, b % 2, h:h + 1])
                last.then_inc(exp_done, 1)

            def att_scale(p, b):
                act.wait_ge(exp_done, CHUNKS * p + b + 1)
                act.wait_ge(rsum_ready, CHUNKS * p + b + 1)
                for h in range(2):
                    c = score[:, b % 2, h, 0:P]
                    last = nc.scalar.activation(c, c, ACT.Copy, scale=rsum[:, b % 2, h:h + 1])
                last.then_inc(p_scaled, 1)

            def att_steps(p, s):
                if 0 <= s - 1 < CHUNKS:
                    att_scale(p, s - 1)
                if s < CHUNKS:
                    att_exp(p, s)

            def phase_a(t, j, extra):
                ph, nxt = Phase("A", t, j), None if t == 1 and isinstance(j, int) else after_a(t, j)
                nc.scalar.copy(cz[:, 0:1], cst[:, bass.ds(C_HEAD + H_ZETA + N_HEAD * j, 1)]).then_inc(zeta_here, 1)
                for s in range(12):
                    if s >= 2 and s % 2 == 0:
                        evacuate(ph, A_UNITS, s // 2 - 1)
                    if s < CHUNKS:
                        if s == 0:
                            act.wait_ge(zeta_here, ph.p + 1)
                        ret_copies(ph.p, s)
                    for step, i in extra.get(s, ()):
                        step(i)
                    if s == 1:
                        split_high(ph, 2, ph.u)
                    if s in (8, 11) and nxt is not None:
                        split_high(nxt, s // 11, ph.group_used(s // 11))
                evacuate(ph, A_UNITS, 5)

            def phase_b(t, j, att_t, att_p):
                ph = Phase("B", t, j)
                nxt = Phase("K", t, 0) if isinstance(j, int) and j == 0 else Phase("A", t, j)
                for s in range(12):
                    if s >= 2 and s % 2 == 0:
                        evacuate(ph, B_UNITS, s // 2 - 1)
                    if att_p is not None:
                        att_steps(att_p, s)
                    elif s < 4:
                        x_high(4 + s)
                        if s == 0:
                            x_square(7)
                        if s == 1:
                            first_high(2)
                    if att_p is None and 3 <= s < 7:
                        x_square(5 + s)
                    if s == 1 and att_p is not None:
                        split_high(ph, 2, ph.u)
                    if s in (8, 11):
                        split_high(nxt, s // 11, ph.group_used(s // 11))
                evacuate(ph, B_UNITS, 5)

            def keep_v(t, sec):
                act.wait_ge(v_turned, nth(t, sec))
                nc.scalar.copy(av_n[:, 1 + PER_SEC * sec:1 + PER_SEC * (sec + 1), :],
                               ps_f[:, :].rearrange("p (b n) -> p b n", n=P)).then_inc(v_kept, 1)

            def phase_k(t):
                ph, nxt = Phase("K", t, 0), Phase("A", t, 0)
                if t == 1:
                    act.wait_ge(att_summed, 4 * CHUNKS)
                    nc.scalar.copy(ak_s[:, :, 0:P], ak_s[:, :, CHUNKS * P:(CHUNKS + 1) * P])
                    nc.scalar.copy(ak_lo[:, 0:P], ak_lo[:, CHUNKS * P:(CHUNKS + 1) * P])
                    nc.scalar.copy(av_n[:, 0, :], av_n[:, CHUNKS, :])
                for s in range(8):
                    if s >= 2 and s % 2 == 0:
                        evacuate(ph, K_UNITS, s // 2 - 1)
                    if s == 5:
                        keep_v(t, 0)
                    if t == 0:
                        if s < 4:
                            x_high(8 + s)
                        if 2 <= s < 6:
                            x_square(10 + s)
                    if s == 1:
                        split_high(nxt, 0, ph.u)
                    if s == 6:
                        split_high(nxt, 1, ph.group_used(0))
                evacuate(ph, K_UNITS, 3)
                keep_v(t, 1)
                if t == 0:
                    act.wait_ge(x_normed, TILES)

            for i in range(3):
                x_square(i)
            x_high(0)
            x_square(3)
            x_high(1)
            first_high(0)
            x_high(2)
            x_square(4)
            x_high(3)
            x_square(5)
            x_square(6)
            first_high(1)
            act.wait_ge(const_in, 32)
            for t in range(2):
                phase_b(t, 0, 0, None if t == 0 else 3)
                phase_k(t)
                with act.Fori(0, HEADS - 1) as j:
                    phase_a(t, j, {})
                    phase_b(t, j + 1, t, 4 * t + j)
                if t == 0:
                    phase_a(0, 3, {6: [(x_high, 12)], 7: [(x_high, 13)], 8: [(x_high, 14)], 10: [(x_high, 15)]})
                else:
                    phase_a(1, 3, {2: [(w_out_high, 0)], 3: [(w_out_high, 1)], 4: [(w_out_high, 2)],
                                   5: [(w_out_high, 3)], 10: [(mix_high, 0)], 11: [(mix_high, 1)]})

            def out_square(n):
                i, c = out_units[n]
                act.wait_ge(out_done, n + 1)
                if i >= 2 and c == 0:
                    act.wait_ge(out_ms, i - 1)
                if n >= 1:
                    act.wait_ge(out_squared, n)
                nc.scalar.activation(out_junk, out_banks[n % 3][:, :], ACT.Square,
                                     accum_out=xss[:, i % 2, c:c + 1]).then_inc(out_squared, 1)

            w_out_high(4)
            w_out_high(5)
            w_out_high(6)
            for n in range(2 * TILES):
                for half in range(2):
                    s = 2 * n + half
                    if s < 12:
                        att_steps(7, s)
                    if half == 0 and n >= 1:
                        out_square(n - 1)
                    if s == 1:
                        w_out_high(7)
                    if s in (3, 7):
                        mix_high(2 + s // 7)
                    if half == 1 and n >= 4 and n % 2 == 0 and n // 2 + 2 < TILES:
                        mix_high(n // 2 + 2)
            out_square(2 * TILES - 1)

        @block.vector
        def _(dve):
            for i, (k, sec) in enumerate((k, sec) for k in ("rg", "ag") for sec in range(2)):
                nc.vector.memset(credit[:, i:i + 1], 0.0).then_inc(stored[k][sec], 16)

            def x_mean(i):
                b = i % 2
                dve.wait_ge(x_squared, i + 1)
                if i >= 2:
                    dve.wait_ge(x_rs, i - 1)
                nc.vector.tensor_scalar(xz[:, b:b + 1], xss[:, b, 0:1], 1.0 / DM, EPS, ALU.mult,
                                        ALU.add).then_inc(x_var, 1)

            def x_norm(i):
                dve.wait_ge(x_rs, i + 1)
                nc.vector.scalar_tensor_tensor(out=xt[:, i % 4, :], in0=xt[:, i % 4, :],
                                               scalar=xr[:, i % 2:i % 2 + 1], in1=gain[:, :],
                                               op0=ALU.mult, op1=ALU.mult).then_inc(x_normed, 1)
                if i + 1 not in (12, TILES):
                    x_mean(i + 1)

            def x_low(i):
                b, at = (i // PER_SEC) % 3, P * (i % PER_SEC)
                for h, bank in enumerate(x_banks(i)):
                    ks = slice(4 * h, 4 * h + 4)
                    dve.wait_ge(x_hi, 2 * i + h + 1)
                    nc.vector.tensor_tensor(big[:, b, 1, ks, at:at + P],
                                            bank[:, :].rearrange("p (k n) -> p k n", n=P),
                                            big[:, b, 0, ks, at:at + P], ALU.subtract).then_inc(x_lo, 1)

            def query_low(p, sec):
                cols = slice(SEC * sec, SEC * (sec + 1))
                bank = proj[A_UNITS.index(("aq", sec)) % 2]
                dve.wait_ge(aq_hi, nth(p, sec))
                for h, rows in enumerate(head_rows):
                    last = nc.vector.scalar_tensor_tensor(out=aq_s[head_rows[1 - h], h, cols], in0=bank[rows, :],
                                                          scalar=0.125, in1=aq_s[rows, h, cols],
                                                          op0=ALU.mult, op1=ALU.subtract)
                last.then_inc(copied["aq"], 1)

            def key_low(t, sec):
                cols = slice(P + SEC * sec, P + SEC * (sec + 1))
                bank = proj[K_UNITS.index(("ak", sec)) % 2]
                dve.wait_ge(ak_hi, nth(t, sec))
                for h, rows in enumerate(head_rows):
                    last = nc.vector.tensor_tensor(ak_lo[rows, cols], bank[rows, :], ak_s[rows, h, cols],
                                                   ALU.subtract)
                last.then_inc(copied["ak"], 1)

            def make_gate(kind, p, sec):
                g = gate[kind][:, SEC * sec:SEC * (sec + 1)]
                bank = proj[A_UNITS.index((kind, sec)) % 2]
                dve.wait_ge(tanh_done[kind], nth(p, sec))
                nc.vector.scalar_tensor_tensor(out=g, in0=g, scalar=1.0, in1=bank[:, :], op0=ALU.add,
                                               op1=ALU.mult).then_inc(gated[kind], 1)

            def combine(kind, p, sec):
                g = gate[kind][:, SEC * sec:SEC * (sec + 1)]
                if kind == "rg":
                    dve.wait_ge(ret_turned, nth(p, sec))
                else:
                    dve.wait_ge(att_summed, CHUNKS * p + PER_SEC * (sec + 1))
                dve.wait_ge(gated[kind], nth(p, sec))
                nc.vector.tensor_tensor(g, turned[sec][:, :], g, ALU.mult).then_inc(combined[kind], 1)

            def load_state(t, j, p):
                if t == 0:
                    nc.vector.memset(state[:, :], 0.0).then_inc(state_ready, 1)
                else:
                    dve.wait_ge(state_saved, HEADS)
                    nc.vector.tensor_copy(state[:, :], state_all[:, bass.ds(j, 1), :]).then_inc(state_ready, 1)

            def ret_mask(p, c):
                dve.wait_ge(ret_scored, CHUNKS * p + c + 1)
                nc.vector.scalar_tensor_tensor(out=p_ret[:, c % 2, :], in0=ps_b[:, 0:P],
                                               scalar=ca[:, H_GCINV2:H_GCINV2 + 1], in1=masks[:, 1, :],
                                               op0=ALU.mult, op1=ALU.mult).then_inc(ret_masked, 1)

            def ret_state(p, c):
                dve.wait_ge(ret_summed, CHUNKS * p + c + 1)
                nc.vector.tensor_copy(o_ret[:, c, :], ps_c[:, 0:P]).then_inc(o_copied, 1)
                dve.wait_ge(state_ready, (CHUNKS + 1) * p + c + 1)
                nc.vector.scalar_tensor_tensor(out=state[:, :], in0=state[:, :], scalar=ca[:, H_GC:H_GC + 1],
                                               in1=ps_c[:, P:2 * P], op0=ALU.mult,
                                               op1=ALU.add).then_inc(state_ready, 1)

            def ret_stats(p, c):
                dve.wait_ge(o_copied, CHUNKS * p + c + 1)
                nc.vector.bn_stats(bn[:, c, :], o_ret[:, c, :]).then_inc(bn_done, 1)
                wait_apart(dve, bn_done, CHUNKS * p + c + 1)
                nc.vector.bn_aggr(mv[:, c, :], bn[:, c, :]).then_inc(aggr_done, 1)

            def ret_var(p, sec):
                cs = slice(PER_SEC * sec, PER_SEC * (sec + 1))
                dve.wait_ge(aggr_done, CHUNKS * p + PER_SEC * (sec + 1))
                nc.vector.tensor_scalar(zvar[:, cs], mv[:, cs, 1], ca[:, H_XI2:H_XI2 + 1], EPS, ALU.mult,
                                        ALU.add).then_inc(var_ready, 1)

            def ret_norm(p, sec):
                cs = slice(PER_SEC * sec, PER_SEC * (sec + 1))
                dve.wait_ge(rvar_ready, nth(p, sec))
                nc.vector.tensor_scalar(rscale[:, cs], rvar[:, cs], ca[:, H_XIH:H_XIH + 1], None,
                                        ALU.mult).then_inc(scale_ready, 1)
                dve.wait_ge(scale_ready, nth(p, sec))
                for c in range(PER_SEC * sec, PER_SEC * (sec + 1)):
                    last = nc.vector.tensor_scalar(o_ret[:, c, :], o_ret[:, c, :], mv[:, c, 0:1],
                                                   rscale[:, c:c + 1], ALU.subtract, ALU.mult)
                last.then_inc(o_normed, 1)

            def att_bias(p, t, b):
                dve.wait_ge(att_scored, CHUNKS * p + b + 1)
                par, alone = b % 2, t == 0 and b == 0
                lo = P if alone else 0
                nc.vector.tensor_copy(score[:, par, :, P], sink[:, :])
                for h in range(2):
                    last = nc.vector.tensor_tensor_reduce(
                        score[:, par, h, 0:P] if alone else biased[:, h, :], (ps_a, ps_b)[h][:, lo:KEYS],
                        bias[:, h, lo:KEYS], 1.0, sink[:, h:h + 1], ALU.add, ALU.max, top[:, par, h:h + 1])
                last.then_inc(att_biased, 1)
                dve.wait_ge(att_biased, CHUNKS * p + b + 1)
                if not alone:
                    nc.vector.tensor_tensor(score[:, par, :, 0:P], biased[:, :, 0:P], biased[:, :, P:KEYS],
                                            ALU.max)
                nc.vector.tensor_scalar(ntop[:, par, :], top[:, par, :], -1.0, None,
                                        ALU.mult).then_inc(max_ready, 1)

            def att_inverse(p, b):
                dve.wait_ge(exp_done, CHUNKS * p + b + 1)
                nc.vector.reciprocal(rsum[:, b % 2, :], esum[:, b % 2, :]).then_inc(rsum_ready, 1)

            def att_mask(p, b):
                dve.wait_ge(p_turned, CHUNKS * p + b + 1)
                nc.vector.tensor_tensor(
                    p_t[:, :, :, :],
                    ps_c[:, 0:2 * P].rearrange("p (h n) -> p h n", h=2).unsqueeze(2).to_broadcast([P, 2, 2, P]),
                    masks.unsqueeze(1).to_broadcast([P, 2, 2, P]), ALU.mult).then_inc(p_masked, 1)

            def att_start(p, j):
                nc.vector.tensor_copy(cb[:, :], cst[:, bass.ds(C_HEAD + N_HEAD * j, N_HEAD)]).then_inc(att_consts, 1)
                nc.vector.tensor_copy(sink[:, :], sink_all[:, :, bass.ds(j, 1)]).then_inc(att_consts, 1)
                dve.wait_ge(att_consts, 2 * p + 2)
                for h in range(2):
                    nc.vector.tensor_scalar(bias[:, h, :], cst[:, C_DIST:C_DIST + KEYS],
                                            cb[:, H_SLOPE + h:H_SLOPE + h + 1], None,
                                            ALU.mult).then_inc(bias_made, 1)
                dve.wait_ge(bias_made, 2 * p + 2)

            def att_steps(p, t, s):
                if 0 <= s - 1 < CHUNKS:
                    att_inverse(p, s - 1)
                if 0 <= s - 2 < CHUNKS:
                    att_mask(p, s - 2)
                if s < CHUNKS:
                    att_bias(p, t, s)
                if s == 7:
                    combine("ag", p, 0)
                if s == 11:
                    combine("ag", p, 1)

            def phase_a(t, j, x_tiles):
                ph = Phase("A", t, j)
                p = ph.p
                nc.vector.tensor_copy(ca[:, :], cst[:, bass.ds(C_HEAD + N_HEAD * j, N_HEAD)]).then_inc(ret_consts, 1)
                load_state(t, j, p)
                dve.wait_ge(ret_consts, p + 1)
                for s in range(12):
                    if s in (2, 8):
                        query_low(p, s // 8)
                    if s == 4:
                        make_gate("rg", p, 0)
                    if s == 6:
                        make_gate("ag", p, 0)
                    if s == 10:
                        make_gate("rg", p, 1)
                    if 0 <= s - 1 < CHUNKS:
                        ret_state(p, s - 1)
                    if s < CHUNKS:
                        ret_mask(p, s)
                    if 0 <= s - 1 < CHUNKS:
                        ret_stats(p, s - 1)
                    if s == 4:
                        ret_var(p, 0)
                    if s == 5:
                        ret_norm(p, 0)
                    if s == 8:
                        ret_var(p, 1)
                        dve.wait_ge(state_ready, (CHUNKS + 1) * (p + 1))
                        combine("rg", p, 0)
                        nc.vector.tensor_copy(state_all[:, bass.ds(j, 1), :], state[:, :]).then_inc(state_saved, 1)
                    if s == 9:
                        ret_norm(p, 1)
                        att_start(p, j)
                    if s in x_tiles:
                        x_low(x_tiles[s])
                make_gate("ag", p, 1)
                combine("rg", p, 1)

            def phase_b(att_t, att_p):
                if att_p is None:
                    for i in range(4, 8):
                        x_low(i)
                        if i + 2 < 8:
                            x_norm(i + 2)
                    for i in range(8, 12):
                        x_norm(i)
                    return
                for s in range(12):
                    att_steps(att_p, att_t, s)

            x_mean(0)
            dve.wait_ge(gain_in, 16)
            x_norm(0)
            x_norm(1)
            for i in range(4):
                x_low(i)
                if i < 2:
                    x_norm(i + 2)
            x_norm(4)
            x_norm(5)
            dve.wait_ge(const_in, 32)
            for t in range(2):
                phase_b(0, None if t == 0 else 3)
                if t == 0:
                    for i in range(8, 12):
                        if i == 11:
                            key_low(0, 0)
                        x_low(i)
                    x_mean(12)
                    for i in range(12, 16):
                        x_norm(i)
                    dve.wait_ge(x_normed, TILES)
                else:
                    key_low(1, 0)
                key_low(t, 1)
                with dve.Fori(0, HEADS - 1) as j:
                    phase_a(t, j, {})
                    phase_b(t, 4 * t + j)
                phase_a(t, 3, {6: 12, 7: 13, 8: 14, 10: 15} if t == 0 else {})

            def w_out_low(q):
                w = IN_GROUPS + q
                hi, lo = w_out_parts(q)
                dve.wait_ge(w_hi, w + 1)
                nc.vector.tensor_tensor(lo, w_out_raw(q), hi, ALU.subtract).then_inc(w_out_ready, 1)

            def out_gain(n):
                i, c = out_units[n]
                cols = slice(SEC * c, SEC * (c + 1))
                dve.wait_ge(out_squared, n + 1)
                if i >= 2 and c == 0:
                    dve.wait_ge(out_stored[i % 2], 16 * (i // 2))
                nc.vector.tensor_tensor(out_sb[i % 2][:, cols], out_banks[n % 3][:, :], gain[:, cols],
                                        ALU.mult).then_inc(out_copied, 1)

            def out_finish(i):
                b, o = i % 2, out_sb[i % 2]
                n = tile_done(i) - 1
                dve.wait_ge(out_squared, n + 1)
                nc.vector.tensor_tensor(xss[:, b, 0:1], xss[:, b, 0:1], xss[:, b, 1:2],
                                        ALU.add).then_inc(out_ms, 1)
                dve.wait_ge(out_ms, i + 1)
                nc.vector.tensor_scalar(xz[:, b:b + 1], xss[:, b, 0:1], 1.0 / DM, EPS, ALU.mult,
                                        ALU.add).then_inc(out_var, 1)
                out_gain(n)
                dve.wait_ge(out_rs, i + 1)
                dve.wait_ge(out_copied, n + 1)
                dve.wait_ge(res_in[i % 4], 16 * (i // 4 + 1))
                parts = [slice(0, DM)] if i < TILES - 1 else [slice(0, SEC), slice(SEC, DM)]
                for cols in parts:
                    nc.vector.scalar_tensor_tensor(out=o[:, cols], in0=o[:, cols], scalar=xr[:, b:b + 1],
                                                   in1=xt[:, i % 4, cols], op0=ALU.mult,
                                                   op1=ALU.add).then_inc(out_added, 1)

            def out_unit(n):
                if out_units[n][1] == 1:
                    out_finish(out_units[n][0])
                else:
                    out_gain(n)

            for s in range(12):
                if s == 2:
                    dve.wait_ge(gain_in, 32)
                att_steps(7, 1, s)
                if s == 0:
                    w_out_low(4)
                    w_out_low(5)
                if s in (1, 2):
                    w_out_low(5 + s)
                if s >= 3 and s % 2 == 1:
                    out_unit((s - 3) // 2)
            for n in range(5, 2 * TILES):
                out_unit(n)

def shape_constants():
    import numpy as np

    c = np.zeros((P, C_ALL), np.float64)
    i = np.arange(P)
    c[:, C_MASK:C_MASK + P] = 0.5 * (i[:, None] > i[None, :])
    c[:, C_MASK + P:C_MASK + 2 * P] = 0.5 * (i[:, None] <= i[None, :])
    dist = i[:, None] + P - np.arange(KEYS)[None, :]
    c[:, C_DIST:C_DIST + KEYS] = np.where((dist >= 0) & (dist < P), -dist, -1e33)
    for j in range(HEADS):
        h = c[:, C_HEAD + N_HEAD * j:C_HEAD + N_HEAD * (j + 1)]
        decay = 1.0 - 2.0 ** (-5.0 - j)
        h[:, H_SLOPE] = 2.0 ** -(j + 1.0)
        h[:, H_SLOPE + 1] = 2.0 ** -(j + 5.0)
        h[:, H_GCINV2] = 2.0 * decay ** -float(P)
        h[:, H_GC] = decay ** float(P)
        h[:, H_XI2] = decay ** (2.0 * (i + 1))
        h[:, H_XIH] = 0.5 * decay ** (i + 1.0)
        h[:, H_ZETA] = decay ** (P - 1.0 - i) * P ** -0.5
    return c.astype(np.float32)


def kernel(x, g_pre, w_in, sinks, w_out, g_post):
    import numpy as np
    import concourse.bacc as bacc
    from concourse.bass_utils import run_bass_kernel_spmd

    nc = bacc.Bacc("TRN2", target_bir_lowering=False, num_devices=1)
    arrays = {"x": np.ascontiguousarray(x).reshape(SEQ, DM), "g_pre": np.ascontiguousarray(g_pre),
              "w_in": np.ascontiguousarray(w_in), "sinks": np.ascontiguousarray(sinks),
              "w_out": np.ascontiguousarray(w_out), "g_post": np.ascontiguousarray(g_post),
              "consts": shape_constants()}
    args = [nc.dram_tensor(n, a.shape, F32, kind="ExternalInput").ap() for n, a in arrays.items()]
    mix = nc.dram_tensor("mix", (TILES, P, 2 * HEADS, P), F32, kind="Internal").ap()
    out = nc.dram_tensor("out", (SEQ, DM), F32, kind="ExternalOutput").ap()
    hybrid_layer(nc, *args, mix, out)
    r = run_bass_kernel_spmd(nc, [arrays], core_ids=[0])
    return r.results[0]["out"].reshape(1, SEQ, DM)
```
